# Optimizing a Trainium2 kernel written in Bass

```python
import math
import jax
import jax.numpy as jnp
from jax import lax
import numpy as np

D_MODEL = 1024
BATCH = 1
SEQ = 128
DEPTH = 1
DEC_BATCH = 1
DEC_SEQ = 1024
PAST_LEN = 128

GRID_W = 64
POS_BASE = 10000.0
EPS = 1e-6
N_MOD = 6
N_DIR = 2
D_MIX = D_MODEL
D_ML = D_MIX // 2
N_ML_HEADS = 4
ML_HEAD = D_ML // N_ML_HEADS
ML_CHUNK = 64
N_GATE = N_DIR * 2 * N_ML_HEADS
D_RG = D_MIX - D_ML
N_RG_BLOCKS = 8
RG_BLOCK = D_RG // N_RG_BLOCKS
RG_C = 8.0
CONV_W = 4
CONV_PAD_LEFT = 2
D_IN = 4 * D_ML + N_GATE + 2 * D_RG
N_EXPERTS = 64
TOP_K = 8
N_GROUPS = 8
TOPK_GROUPS = 4
D_EXPERT = 256
D_SHARED = 256
ROUTED_SCALE = 2.5
MOE_BLOCK = 128

kernel_name = 'hybrid_mlstm_rglru_moe_diffusion_step'

def rmsnorm(x, g):
    xf = x.astype(jnp.float32)
    y = xf * lax.rsqrt(jnp.mean(xf * xf, axis=-1, keepdims=True) + EPS)
    return (y * g.astype(jnp.float32)).astype(x.dtype)

def grid_pos_embed(n_tokens, dim):
    rows_n = n_tokens // GRID_W
    row = jnp.repeat(jnp.arange(rows_n), GRID_W).astype(jnp.float32)
    col = jnp.tile(jnp.arange(GRID_W), rows_n).astype(jnp.float32)
    quarter = dim // 4
    omega = 1.0 / (POS_BASE ** (jnp.arange(quarter, dtype=jnp.float32) / quarter))
    ra = row[:, None] * omega
    ca = col[:, None] * omega
    return jnp.concatenate([jnp.sin(ra), jnp.cos(ra), jnp.sin(ca), jnp.cos(ca)], axis=-1)

def dwconv_centred(x, w, b):
    T = x.shape[1]
    xp = jnp.pad(x, ((0, 0), (CONV_PAD_LEFT, CONV_W - 1 - CONV_PAD_LEFT), (0, 0)))
    y = b
    for j in range(CONV_W):
        y = y + xp[:, j:j + T] * w[j]
    return y

def mlstm_chunked(q, k, v, ig, lf, C0, n0, m0):
    B, H, T, dh = q.shape
    nc = T // ML_CHUNK

    def to_chunks(a):
        return jnp.moveaxis(a.reshape((B, H, nc, ML_CHUNK) + a.shape[3:]), 2, 0)

    causal = jnp.tril(jnp.ones((ML_CHUNK, ML_CHUNK), dtype=bool))

    def step(carry, inp):
        C, n, m = carry
        qb, kb, vb, ib, fb = inp
        b = jnp.cumsum(fb, axis=-1)
        log_d = jnp.where(causal, b[..., :, None] - b[..., None, :] + ib[..., None, :], -jnp.inf)
        inter = b + m[..., None]
        m_t = jnp.maximum(inter, jnp.max(log_d, axis=-1))
        s = jnp.einsum('bhtd,bhsd->bhts', qb, kb) * jnp.exp(log_d - m_t[..., None])
        w_inter = jnp.exp(inter - m_t)
        num = w_inter[..., None] * jnp.einsum('bhtd,bhde->bhte', qb, C) + jnp.einsum('bhts,bhse->bhte', s, vb)
        den = w_inter * jnp.einsum('bhtd,bhd->bht', qb, n) + jnp.sum(s, axis=-1)
        h = num / jnp.maximum(jnp.abs(den), jnp.exp(-m_t))[..., None]
        b_last = b[..., -1]
        log_w = b_last[..., None] - b + ib
        m_new = jnp.maximum(b_last + m, jnp.max(log_w, axis=-1))
        w_s = jnp.exp(log_w - m_new[..., None])
        decay = jnp.exp(b_last + m - m_new)
        C_new = decay[..., None, None] * C + jnp.einsum('bhs,bhsd,bhse->bhde', w_s, kb, vb)
        n_new = decay[..., None] * n + jnp.einsum('bhs,bhsd->bhd', w_s, kb)
        return (C_new, n_new, m_new), h

    (C, n, m), hc = lax.scan(step, (C0, n0, m0), tuple(to_chunks(a) for a in (q, k, v, ig, lf)))
    h = jnp.moveaxis(hc, 0, 2).reshape(B, H, T, dh)
    return h, C, n, m

def mlstm_bidir(q, k, v, ig, lf, C0, n0, m0):
    h_f, Cf, nf, mf = mlstm_chunked(q, k, v, ig[:, 0], lf[:, 0], C0[:, 0], n0[:, 0], m0[:, 0])
    fl = lambda a: jnp.flip(a, axis=2)
    h_b, Cb, nb, mb = mlstm_chunked(fl(q), fl(k), fl(v), fl(ig[:, 1]), fl(lf[:, 1]), C0[:, 1], n0[:, 1], m0[:, 1])
    h = h_f + fl(h_b)
    return h, jnp.stack([Cf, Cb], axis=1), jnp.stack([nf, nb], axis=1), jnp.stack([mf, mb], axis=1)

def _lin_rec(e1, e2):
    a1, b1 = e1
    a2, b2 = e2
    return a1 * a2, a2 * b1 + b2

def rglru_dir(x, wa, ba, wx, bx, lam, h0):
    B, T, _ = x.shape
    xb = x.reshape(B, T, N_RG_BLOCKS, RG_BLOCK)
    r = jax.nn.sigmoid(jnp.einsum('btni,nij->btnj', xb, wa.astype(jnp.float32)).reshape(B, T, D_RG) + ba.astype(jnp.float32))
    i = jax.nn.sigmoid(jnp.einsum('btni,nij->btnj', xb, wx.astype(jnp.float32)).reshape(B, T, D_RG) + bx.astype(jnp.float32))
    log_a = -RG_C * r * jax.nn.softplus(-lam.astype(jnp.float32))
    a = jnp.exp(log_a)
    u = jnp.sqrt(-jnp.expm1(2.0 * log_a)) * (i * x)
    u = u.at[:, 0].add(a[:, 0] * h0)
    _, h = lax.associative_scan(_lin_rec, (a, u), axis=1)
    return h, h[:, -1]

def moe(x2d, router_w, router_bias, exp_w1, exp_w3, exp_w2, shared_w1, shared_w3, shared_w2):
    N, D = x2d.shape
    s = jax.nn.sigmoid(x2d.astype(jnp.float32) @ router_w.astype(jnp.float32))
    sb = s + router_bias.astype(jnp.float32)
    grp = sb.reshape(N, N_GROUPS, N_EXPERTS // N_GROUPS)
    gscore = jnp.sum(lax.top_k(grp, 2)[0], axis=-1)
    _, gidx = lax.top_k(gscore, TOPK_GROUPS)
    gmask = jnp.sum(jax.nn.one_hot(gidx, N_GROUPS, dtype=jnp.float32), axis=1)
    emask = jnp.repeat(gmask, N_EXPERTS // N_GROUPS, axis=1) > 0
    _, eidx = lax.top_k(jnp.where(emask, sb, -jnp.inf), TOP_K)
    wts = jnp.take_along_axis(s, eidx, axis=1)
    wts = wts / jnp.sum(wts, axis=-1, keepdims=True) * ROUTED_SCALE
    S = N * TOP_K
    flat_e = eidx.reshape(S)
    flat_tok = jnp.repeat(jnp.arange(N, dtype=jnp.int32), TOP_K)
    flat_w = wts.reshape(S)
    order = jnp.argsort(flat_e)
    e_sorted = flat_e[order]
    counts = jnp.bincount(flat_e, length=N_EXPERTS)
    padded = (counts + MOE_BLOCK - 1) // MOE_BLOCK * MOE_BLOCK
    start = jnp.cumsum(counts) - counts
    pstart = jnp.cumsum(padded) - padded
    dest = pstart[e_sorted] + jnp.arange(S) - start[e_sorted]
    NB = -(-S // MOE_BLOCK) + N_EXPERTS
    P = NB * MOE_BLOCK
    slot_tok = jnp.zeros((P,), jnp.int32).at[dest].set(flat_tok[order])
    slot_w = jnp.zeros((P,), jnp.float32).at[dest].set(flat_w[order])
    block_end = jnp.cumsum(padded) // MOE_BLOCK
    block_expert = jnp.minimum(jnp.searchsorted(block_end, jnp.arange(NB), side='right'), N_EXPERTS - 1)

    def expert_block(args):
        tok, e = args
        xb = x2d[tok]
        hb = jax.nn.silu(xb @ exp_w1[e]) * (xb @ exp_w3[e])
        return hb @ exp_w2[e]

    yb = lax.map(expert_block, (slot_tok.reshape(NB, MOE_BLOCK), block_expert))
    routed = jax.ops.segment_sum(yb.reshape(P, D) * slot_w[:, None].astype(x2d.dtype), slot_tok, num_segments=N)
    shared = (jax.nn.silu(x2d @ shared_w1) * (x2d @ shared_w3)) @ shared_w2
    return routed + shared

def trunk_layer(x, mod, C0, n0, m0, h0, lp):
    B, T, _ = x.shape
    mod = mod.astype(x.dtype)
    sh1, sc1, g1, sh2, sc2, g2 = [mod[:, j][:, None, :] for j in range(N_MOD)]
    hn = rmsnorm(x, lp['norm1']) * (1 + sc1) + sh1
    z = (hn @ lp['w_in']).astype(jnp.float32)
    cuts = [D_ML, 2 * D_ML, 3 * D_ML, 4 * D_ML, 4 * D_ML + N_GATE, 4 * D_ML + N_GATE + D_RG]
    q, k, v, o, gt, xr, gr = jnp.split(z, cuts, axis=-1)

    def heads(a):
        return a.reshape(B, T, N_ML_HEADS, ML_HEAD).transpose(0, 2, 1, 3)
    q, k, v = heads(q), heads(k) * (ML_HEAD ** -0.5), heads(v)
    gt = gt.reshape(B, T, N_DIR, 2, N_ML_HEADS) + lp['mlstm_gate_bias'].astype(jnp.float32)
    gt = gt.transpose(0, 2, 3, 4, 1)
    ig = gt[:, :, 0]
    lf = jax.nn.log_sigmoid(gt[:, :, 1])
    h_ml, C, n, m = mlstm_bidir(q, k, v, ig, lf, C0.astype(jnp.float32), n0.astype(jnp.float32), m0.astype(jnp.float32))
    h_ml = h_ml * lax.rsqrt(jnp.mean(h_ml * h_ml, axis=-1, keepdims=True) + EPS)
    y_ml = h_ml.transpose(0, 2, 1, 3).reshape(B, T, D_ML) * lp['mlstm_norm'].astype(jnp.float32) * jax.nn.sigmoid(o)

    xr = dwconv_centred(xr, lp['rg_conv_w'].astype(jnp.float32), lp['rg_conv_b'].astype(jnp.float32))
    h0f = h0.astype(jnp.float32)
    hr_f, hfin_f = rglru_dir(xr, lp['rg_wa'][0], lp['rg_ba'][0], lp['rg_wx'][0], lp['rg_bx'][0], lp['rg_lambda'][0], h0f[:, 0])
    hr_b, hfin_b = rglru_dir(jnp.flip(xr, 1), lp['rg_wa'][1], lp['rg_ba'][1], lp['rg_wx'][1], lp['rg_bx'][1], lp['rg_lambda'][1], h0f[:, 1])
    y_rg = rmsnorm(hr_f + jnp.flip(hr_b, 1), lp['rg_norm']) * jax.nn.gelu(gr)

    mix = jnp.concatenate([y_ml, y_rg], axis=-1).astype(x.dtype) @ lp['w_out']
    x = x + g1 * mix

    hn2 = rmsnorm(x, lp['norm2']) * (1 + sc2) + sh2
    y = moe(hn2.reshape(B * T, D_MODEL), lp['router_w'], lp['router_bias'], lp['exp_w1'], lp['exp_w3'],
            lp['exp_w2'], lp['shared_w1'], lp['shared_w3'], lp['shared_w2']).reshape(B, T, D_MODEL)
    x = x + g2 * y
    h_fin = jnp.stack([hfin_f, hfin_b], axis=1)
    return x, C, n, m, h_fin

def setup_inputs(seed: int = 0) -> dict:
    key = jax.random.key(seed)
    ks = jax.random.split(key, 34)

    def nrm(k, shape, scale):
        return jax.random.normal(k, shape, jnp.float32) * scale

    gate_base = jnp.stack([jnp.zeros((N_ML_HEADS,), jnp.float32),
                           jnp.linspace(3.0, 6.0, N_ML_HEADS, dtype=jnp.float32)])
    u = jax.random.uniform(ks[20], (DEPTH, N_DIR, D_RG), jnp.float32, minval=0.9, maxval=0.999)
    return {
        'x_prompt': nrm(ks[0], (BATCH, SEQ, D_MODEL), 1.0),
        'x_sample': nrm(ks[1], (DEC_BATCH, DEC_SEQ, D_MODEL), 1.0),
        'c': nrm(ks[2], (DEC_BATCH, D_MODEL), 1.0),
        'state_mlstm_C': nrm(ks[3], (DEC_BATCH, DEPTH, N_DIR, N_ML_HEADS, ML_HEAD, ML_HEAD), 0.05),
        'state_mlstm_n': nrm(ks[4], (DEC_BATCH, DEPTH, N_DIR, N_ML_HEADS, ML_HEAD), 0.05),
        'state_mlstm_m': nrm(ks[5], (DEC_BATCH, DEPTH, N_DIR, N_ML_HEADS), 1.0),
        'state_rglru_h': nrm(ks[6], (DEC_BATCH, DEPTH, N_DIR, D_RG), 0.5),
        'c_ctx': nrm(ks[7], (D_MODEL,), 1.0),
        'w_ada': nrm(ks[8], (DEPTH, D_MODEL, N_MOD * D_MODEL), 0.5 * D_MODEL ** -0.5),
        'b_ada': nrm(ks[9], (DEPTH, N_MOD * D_MODEL), 0.02),
        'norm1': 1.0 + nrm(ks[10], (DEPTH, D_MODEL), 0.02),
        'w_in': nrm(ks[11], (DEPTH, D_MODEL, D_IN), D_MODEL ** -0.5),
        'mlstm_gate_bias': nrm(ks[12], (DEPTH, N_DIR, 2, N_ML_HEADS), 0.1) + gate_base[None, None],
        'mlstm_norm': 1.0 + nrm(ks[13], (DEPTH, D_ML), 0.02),
        'rg_conv_w': nrm(ks[14], (DEPTH, CONV_W, D_RG), CONV_W ** -0.5),
        'rg_conv_b': nrm(ks[15], (DEPTH, D_RG), 0.02),
        'rg_wa': nrm(ks[16], (DEPTH, N_DIR, N_RG_BLOCKS, RG_BLOCK, RG_BLOCK), RG_BLOCK ** -0.5),
        'rg_ba': nrm(ks[17], (DEPTH, N_DIR, D_RG), 0.02),
        'rg_wx': nrm(ks[18], (DEPTH, N_DIR, N_RG_BLOCKS, RG_BLOCK, RG_BLOCK), RG_BLOCK ** -0.5),
        'rg_bx': nrm(ks[19], (DEPTH, N_DIR, D_RG), 0.02),
        'rg_lambda': jnp.log(u) - jnp.log1p(-u),
        'rg_norm': 1.0 + nrm(ks[21], (DEPTH, D_RG), 0.02),
        'w_out': nrm(ks[22], (DEPTH, D_MIX, D_MODEL), D_MIX ** -0.5),
        'norm2': 1.0 + nrm(ks[23], (DEPTH, D_MODEL), 0.02),
        'router_w': nrm(ks[24], (DEPTH, D_MODEL, N_EXPERTS), D_MODEL ** -0.5),
        'router_bias': nrm(ks[25], (DEPTH, N_EXPERTS), 0.01),
        'exp_w1': nrm(ks[26], (DEPTH, N_EXPERTS, D_MODEL, D_EXPERT), D_MODEL ** -0.5),
        'exp_w3': nrm(ks[27], (DEPTH, N_EXPERTS, D_MODEL, D_EXPERT), D_MODEL ** -0.5),
        'exp_w2': nrm(ks[28], (DEPTH, N_EXPERTS, D_EXPERT, D_MODEL), D_EXPERT ** -0.5),
        'shared_w1': nrm(ks[29], (DEPTH, D_MODEL, D_SHARED), D_MODEL ** -0.5),
        'shared_w3': nrm(ks[30], (DEPTH, D_MODEL, D_SHARED), D_MODEL ** -0.5),
        'shared_w2': nrm(ks[31], (DEPTH, D_SHARED, D_MODEL), D_SHARED ** -0.5),
        'norm_final': 1.0 + nrm(ks[32], (D_MODEL,), 0.02),
    }

def reference(x_prompt, x_sample, c, state_mlstm_C, state_mlstm_n, state_mlstm_m, state_rglru_h, c_ctx,
              w_ada, b_ada, norm1, w_in, mlstm_gate_bias, mlstm_norm, rg_conv_w, rg_conv_b, rg_wa, rg_ba,
              rg_wx, rg_bx, rg_lambda, rg_norm, w_out, norm2, router_w, router_bias, exp_w1, exp_w3, exp_w2,
              shared_w1, shared_w3, shared_w2, norm_final):
    bp = x_prompt.shape[0]
    bs = x_sample.shape[0]
    xp = x_prompt
    xs = x_sample + grid_pos_embed(x_sample.shape[1], D_MODEL).astype(x_sample.dtype)[None]
    zC = jnp.zeros((bp, N_DIR, N_ML_HEADS, ML_HEAD, ML_HEAD), jnp.float32)
    zn = jnp.zeros((bp, N_DIR, N_ML_HEADS, ML_HEAD), jnp.float32)
    zm = jnp.zeros((bp, N_DIR, N_ML_HEADS), jnp.float32)
    zh = jnp.zeros((bp, N_DIR, D_RG), jnp.float32)
    new_C, new_n, new_m, new_h = [], [], [], []
    for l in range(DEPTH):
        lp = {
            'norm1': norm1[l], 'w_in': w_in[l], 'mlstm_gate_bias': mlstm_gate_bias[l], 'mlstm_norm': mlstm_norm[l],
            'rg_conv_w': rg_conv_w[l], 'rg_conv_b': rg_conv_b[l], 'rg_wa': rg_wa[l], 'rg_ba': rg_ba[l],
            'rg_wx': rg_wx[l], 'rg_bx': rg_bx[l], 'rg_lambda': rg_lambda[l], 'rg_norm': rg_norm[l],
            'w_out': w_out[l], 'norm2': norm2[l], 'router_w': router_w[l], 'router_bias': router_bias[l],
            'exp_w1': exp_w1[l], 'exp_w3': exp_w3[l], 'exp_w2': exp_w2[l],
            'shared_w1': shared_w1[l], 'shared_w3': shared_w3[l], 'shared_w2': shared_w2[l],
        }
        mod_ctx = (jax.nn.silu(c_ctx) @ w_ada[l] + b_ada[l]).reshape(1, N_MOD, D_MODEL)
        mod_lat = (jax.nn.silu(c) @ w_ada[l] + b_ada[l]).reshape(bs, N_MOD, D_MODEL)
        xp, Cc, nc, mc, hc = trunk_layer(xp, mod_ctx, zC, zn, zm, zh, lp)
        new_C.append(Cc)
        new_n.append(nc)
        new_m.append(mc)
        new_h.append(hc)
        xs, _, _, _, _ = trunk_layer(xs, mod_lat, state_mlstm_C[:, l], state_mlstm_n[:, l],
                                     state_mlstm_m[:, l], state_rglru_h[:, l], lp)
    y_prompt = rmsnorm(xp, norm_final)
    y_sample = rmsnorm(xs, norm_final)
    new_mlstm_C = jnp.stack(new_C, axis=1)
    new_mlstm_n = jnp.stack(new_n, axis=1)
    new_mlstm_m = jnp.stack(new_m, axis=1)
    new_rglru_h = jnp.stack(new_h, axis=1)
    return (y_prompt, y_sample, new_mlstm_C, new_mlstm_n, new_mlstm_m, new_rglru_h)


_drawn_inputs = setup_inputs


def setup_inputs(seed=0):
    import zlib

    import numpy as np

    out = dict(_drawn_inputs(seed))
    spreads = {}
    factors = {'state_mlstm_C': 5.43,
     'state_mlstm_n': 8.0,
     'state_mlstm_m': 7.384,
     'state_rglru_h': 6.531,
     'mlstm_norm': 22.886,
     'rg_ba': 8.0,
     'rg_bx': 7.72,
     'rg_norm': 18.526,
     'norm_final': 7.453,
     'norm2': 3.096}
    for name, (base, spread) in spreads.items():
        noise = np.random.default_rng([zlib.crc32(name.encode()), seed]).standard_normal(out[name].shape)
        drawn = base * np.exp(spread * noise) if base else spread * noise
        out[name] = jnp.asarray(drawn.astype(out[name].dtype))
    for name, factor in factors.items():
        out[name] = (out[name] * factor).astype(out[name].dtype)
    return out
```

```python
from contextlib import ExitStack

import concourse.bass as bass
from concourse import mybir

F32 = mybir.dt.float32
BF16 = mybir.dt.bfloat16
F32R = mybir.dt.float32r
I32 = mybir.dt.int32
ALU = mybir.AluOpType
ACT = mybir.ActivationFunctionType
AX = mybir.AxisListType.X

P = 128
D = 1024
KT = D // P
NCTX, NLAT = 128, 1024
N = NCTX + NLAT
NT = N // P
SPANS = [(0, NCTX), (NCTX, 512), (NCTX + 512, 512)]
SEGS = [(0, NCTX), (NCTX, NLAT)]
H = 4
DML = H * P
DRG = D - DML
RT = DRG // P
QC, KC, VC, OC, GC = 0, DML, 2 * DML, 3 * DML, 4 * DML
XC, RC = GC + 16, GC + 16 + DRG
EPS = 1e-6
BIG = 1e30
NE, NGRP, DE = 64, 8, 256
NX = NE + 1
ROWS = N + P
TABLE = 160
WSLOT = 3
RS_MAGIC = 1597463007.0

C_ID, C_TRI, C_IOTA, C_NEGF, C_NEGB = 0, P, 2 * P, 3 * P, 4 * P
C_SEL = 5 * P
C_ONE = C_SEL + H * P
C_SLOT = C_ONE + P
C_TOK = C_SLOT + 4
C_BLK = C_TOK + NT
C_EPS = C_BLK + 2
C_END = C_EPS + 1


def shape_constants():
    import numpy as np
    p = np.arange(P, dtype=np.float32)
    c = np.zeros((P, C_END), np.float32)
    c[:, C_ID:C_ID + P] = np.eye(P)
    c[:, C_TRI:C_TRI + P] = p[:, None] < p[None, :]
    c[:, C_IOTA:C_IOTA + P] = p[None, :]
    c[:, C_NEGF:C_NEGF + P] = np.where(p[:, None] <= p[None, :], 0.0, -BIG)
    c[:, C_NEGB:C_NEGB + P] = np.where(p[:, None] >= p[None, :], 0.0, -BIG)
    for h in range(H):
        c[h, C_SEL + h * P:C_SEL + (h + 1) * P] = 1.0
    c[:, C_ONE:C_ONE + P] = 1.0
    c[:, C_SLOT] = -p
    c[:, C_SLOT + 1] = N + p
    c[:, C_SLOT + 2] = p
    for t in range(NT):
        c[:, C_TOK + t] = P * t - N
    c[:, C_BLK] = p
    c[:, C_EPS] = EPS
    c[:, C_BLK + 1] = P + p
    quarter = D // 4
    omega = (1.0 / (10000.0 ** (np.arange(quarter, dtype=np.float32) / np.float32(quarter)))).astype(np.float32)
    ra = np.arange(NLAT // 64, dtype=np.float32)[:, None] * omega
    ca = np.arange(64, dtype=np.float32)[:, None] * omega
    row = np.concatenate([np.sin(ra), np.cos(ra)], -1).astype(np.float32)
    col = np.concatenate([np.sin(ca), np.cos(ca)], -1).astype(np.float32)
    return c, row, col


class Chain:

    def __init__(self, eng, sem):
        self.eng, self.sem, self.n = eng, sem, 0

    def __call__(self, ins):
        self.n += 1
        ins.then_inc(self.sem, 1)
        self.eng.wait_ge(self.sem, self.n)


def feat(ap):
    return ap.rearrange("(i p) -> p i", p=P)


def small_loads(a, m):
    loads = [
        (m.cst[:, :], a["consts"]),
        (m.n1row[:, :], a["norm1"].to_broadcast([P, D])),
        (m.gbias[:, :], a["mlstm_gate_bias"][0].rearrange("d g h -> h (d g)")),
        (m.mlnc[:, :], feat(a["mlstm_norm"][0])),
        (m.rgnc[:, :], feat(a["rg_norm"][0])),
        (m.convb[:, :], feat(a["rg_conv_b"][0])),
        (m.m0[:, :], a["state_mlstm_m"][0, 0].rearrange("d h -> h d")),
        (m.wgate[:, :, :], a["w_in"][0].rearrange("(k p) n -> p k n", p=P)[:, :, GC:GC + 16]),
    ]
    for d in range(2):
        loads += [
            (m.lam[:, d * RT:(d + 1) * RT], feat(a["rg_lambda"][0, d])),
            (m.bgate[:, 0, d, :], feat(a["rg_ba"][0, d])),
            (m.bgate[:, 1, d, :], feat(a["rg_bx"][0, d])),
            (m.h0c[:, d, :], feat(a["state_rglru_h"][0, 0, d])),
        ]
    for j in range(4):
        loads.append((m.convw[:, j, :], feat(a["rg_conv_w"][0, j])))
    return loads


class Ring:

    def __init__(self, eng, banks, done, free):
        self.eng, self.banks, self.done, self.free, self.n = eng, banks, done, free, 0

    def fill(self):
        if self.n >= len(self.banks):
            self.eng.wait_ge(self.free, self.n - len(self.banks) + 1)
        return self.banks[self.n % len(self.banks)]

    def filled(self, ins):
        ins.then_inc(self.done, 1)
        self.n += 1

    def drain(self):
        self.eng.wait_ge(self.done, self.n + 1)
        return self.banks[self.n % len(self.banks)]

    def drained(self, ins):
        ins.then_inc(self.free, 1)
        self.n += 1


def newton_rsqrt(link, dve, x, y, t, i32):
    link(dve.tensor_scalar(i32, x.bitcast(I32), 1, None, ALU.logical_shift_right))
    link(dve.tensor_scalar(y.bitcast(I32), i32, -1.0, RS_MAGIC, ALU.mult, ALU.add))
    link(dve.tensor_scalar(x, x, -0.5, None, ALU.mult))
    for _ in range(4):
        link(dve.tensor_tensor(t, y, y, ALU.mult))
        link(dve.tensor_tensor(t, t, x, ALU.mult))
        link(dve.scalar_tensor_tensor(y, t, 1.5, y, ALU.add, ALU.mult))


class Bag:
    pass


def stage_norm1(nc, a, m):
    with ExitStack() as ctx:
        sb = lambda name, shape, dt=F32: ctx.enter_context(nc.sbuf_tensor(name, shape, dt))
        sem = lambda name: ctx.enter_context(nc.semaphore(name))
        NA = 3
        wada = [sb(f"wada{j}", [P, KT, 512]) for j in range(NA)]
        bada = [sb(f"bada{j}", [2, 512]) for j in range(2)]
        mrow = [sb(f"mrow{j}", [2, 512]) for j in range(2)]
        ccs = sb("ccs", [P, KT, 2])
        cct = sb("cct", [P, 2, KT])
        scale = [sb(f"scale1_{s}", [P, D]) for s in range(2)]
        shift = [sb(f"shift1_{s}", [P, D]) for s in range(2)]
        m.n1row = sb("n1row", [P, D])
        m.wgate = sb("wgate", [P, KT, 16])
        m.cc = sb("cc", [P, 2, KT])
        m.posc = sb("posc", [P, 512])
        PS = 3
        posr = [sb(f"posr{j}", [P, 512]) for j in range(PS)]
        x = [sb(f"x{j}", [P, D]) for j in range(NT - 3)] + [m.yT[:, 4 + j, 0:D] for j in range(3)]
        hn = [sb(f"hn{j}", [P, D]) for j in range(2)]
        sq = m.yT[:, 7, 0:D]
        ss, rs, rt = sb("ss1", [P, NT]), sb("rs1", [P, NT]), sb("rt1", [P, NT])
        ri = sb("ri1", [P, NT], I32)
        gtok = sb("gtok", [P, NT, 16])
        s_ada = [sem(f"ld_ada{j}") for j in range(NA)]
        s_bada = [sem(f"ld_bada{j}") for j in range(2)]
        s_modld = sem("ld_modrows1")
        s_x = [sem(f"ld_x{j}") for j in range(NT)]
        s_x1, s_posc = sem("st_x1"), sem("ld_posc")
        s_cc = sem("ld_cc")
        ring_banks = m.banks[0:4]
        e_cc, silu_c = sem("exp_cc"), sem("silu_c")
        full, free = sem("full1"), sem("free1")
        mod_row = sem("mod_row")
        dch = sem("dve_chain1")
        x_pos, x_sq, x_hn = (sem(n) for n in ("x_pos", "x_sq", "x_hn"))
        w_ada = a["w_ada"][0].rearrange("(p k) n -> p k n", k=KT)
        NG = 12
        small = small_loads(a, m)
        m.ld_all = 16 * len(small)
        FIRST = 7
        TAKE = {1: [0], 2: [1], 3: [2], 4: [3], 5: [4, 5], 6: [6, 7, 8]}
        seq = [("mod", g) for g in range(FIRST)]
        for t in range(NT + 1):
            if t < NT:
                seq.append(("turn", t))
            if t >= 1:
                seq.append(("gate_turn", t - 1))
            if FIRST + t < NG:
                seq.append(("mod", FIRST + t))
            if t < NT:
                seq.append(("gate", t))
        jobs_before, n = {}, 0
        for item in seq:
            jobs_before[item] = n
            n += 2 if item[0] == "turn" else 1

        block = ctx.enter_context(nc.Block())

        @block.sync
        def _(sp):
            sp.wait_ge(s_cc, 32)
            for g in range(NG):
                if g >= NA:
                    sp.wait_ge(full, jobs_before["mod", g - NA] + 1)
                sp.dma_start(wada[g % NA][:, :, :], w_ada[:, :, g * 512:(g + 1) * 512]).then_inc(s_ada[g % NA], 16)
                if g == 5:
                    for j in range(2):
                        sp.wait_ge(m.modst[j], 32)
                    for s in range(2):
                        sp.dma_start(shift[s][:, :], m.mods[s:s + 1, 0:D].to_broadcast([P, D])).then_inc(s_modld, 16)
                        sp.dma_start(scale[s][:, :], m.mods[s:s + 1, D:2 * D].to_broadcast([P, D])).then_inc(s_modld, 16)
            for j in range(2):
                sp.wait_ge(m.modst[j], 16 * NG // 2)

        @block.gpsimd
        def _(pool):
            for b in range(2):
                pool.dma_start(m.posc[64 * b:64 * b + 64, :], a["pos_col"]).then_inc(s_posc, 16)
            for t in range(NT):
                src = a["x_prompt"][0] if t == 0 else a["x_sample"][0, (t - 1) * P:t * P, :]
                pool.dma_start(x[t][:, :], src).then_inc(s_x[t], 16)
                if t >= 1:
                    if t > PS:
                        pool.wait_ge(x_pos, t - PS + 1)
                    r = 2 * (t - 1)
                    pool.dma_start(posr[t % PS][:, :], a["pos_row"][r:r + 2, :].unsqueeze(1).to_broadcast([2, 64, 512])).then_inc(s_x[t], 16)
                for dst, src in small[3 * t:3 * t + 3]:
                    pool.dma_start(dst, src, allow_slow_non_contiguous=True).then_inc(m.ld, 16)
            for t in range(NT):
                pool.wait_ge(x_hn, t + 1)
                pool.dma_start(m.x1[t * P:(t + 1) * P, :], x[t][:, :]).then_inc(s_x1, 16)
            pool.wait_ge(s_x1, 16 * NT)

        @block.tensor
        def _(pe):
            ring = Ring(pe, ring_banks, full, free)
            pe.wait_ge(silu_c, 1)
            for kind, t in seq:
                if kind == "mod":
                    bank = ring.fill()
                    pe.wait_ge(s_ada[t % NA], 16 * (t // NA + 1))
                    for k in range(KT):
                        mm = pe.matmul(bank[0:2, :], ccs[:, k, :], wada[t % NA][:, k, :], start=(k == 0), stop=(k == KT - 1))
                    ring.filled(mm)
                elif kind == "turn":
                    if t == 0:
                        pe.wait_ge(m.ld, m.ld_all)
                    pe.wait_ge(x_hn, t + 1)
                    for half in range(2):
                        bank = ring.fill()
                        for k in range(4):
                            kk = 4 * half + k
                            mm = pe.transpose(bank[:, k * P:(k + 1) * P], hn[t % 2][:, kk * P:(kk + 1) * P], m.ident)
                        ring.filled(mm)
                elif kind == "gate":
                    bank = ring.fill()
                    pe.wait_ge(free, jobs_before["turn", t] + 2)
                    for k in range(KT):
                        mm = pe.matmul(bank[:, 0:16], m.hnT[:, k, t * P:(t + 1) * P], m.wgate[:, k, :],
                                       start=(k == 0), stop=(k == KT - 1))
                    ring.filled(mm)
                else:
                    bank = ring.fill()
                    pe.wait_ge(free, jobs_before["gate", t] + 1)
                    for g in range(4):
                        mm = pe.transpose(bank[0:H, g * P:(g + 1) * P], gtok[:, t, 4 * g:4 * g + 4], m.ident)
                    ring.filled(mm)

        @block.scalar
        def _(act):
            ring = Ring(act, ring_banks, full, free)
            act.dma_start(m.cc[:, 0, :], a["c_ctx"].rearrange("(p k) -> p k", k=KT)).then_inc(s_cc, 16)
            act.dma_start(m.cc[:, 1, :], a["c"][0].rearrange("(p k) -> p k", k=KT)).then_inc(s_cc, 16)

            def load_bias(g):
                act.dma_start(bada[g % 2][:, :],
                              a["b_ada"][:, g * 512:(g + 1) * 512].to_broadcast([2, 512])).then_inc(s_bada[g % 2], 16)

            def store_row(g):
                act.wait_ge(mod_row, g + 1)
                act.dma_start(m.mods[:, g * 512:(g + 1) * 512], mrow[g % 2][:, :]).then_inc(m.modst[g % 2], 16)
                if g + 2 < NG:
                    load_bias(g + 2)

            load_bias(0)
            load_bias(1)
            act.wait_ge(s_cc, 32)
            act.activation(cct[:, :, :], m.cc[:, :, :], ACT.Exp, scale=-1.0).then_inc(e_cc, 1)

            def squares(t):
                act.wait_ge(x_pos, t + 1)
                if t >= 1:
                    act.wait_ge(x_sq, t)
                act.activation(sq, x[t][:, :], ACT.Square, accum_out=ss[:, t:t + 1]).then_inc(x_sq, 1)

            for kind, t in seq:
                if kind == "mod":
                    if t >= 1:
                        store_row(t - 1)
                    bank = ring.drain()
                    if t >= 2:
                        act.wait_ge(m.modst[t % 2], 16 * (t // 2))
                    ring.drained(act.activation(mrow[t % 2][:, :], bank[0:2, :], ACT.Copy))
                    for tt in TAKE.get(t, []):
                        squares(tt)
                elif kind == "turn":
                    for half in range(2):
                        bank = ring.drain()
                        ring.drained(act.activation(m.hnT[:, 4 * half:4 * half + 4, t * P:(t + 1) * P],
                                                    bank[:, :].rearrange("p (k n) -> p k n", k=4), ACT.Copy))
                elif kind == "gate":
                    bank = ring.drain()
                    ring.drained(act.activation(gtok[:, t, :], bank[:, 0:16], ACT.Copy))
                else:
                    if t == NG - FIRST:
                        store_row(NG - 1)
                    bank = ring.drain()
                    if t == 0:
                        act.wait_ge(m.ld, m.ld_all)
                    for g in range(4):
                        ins = act.activation(m.g4[:, g, t * P:(t + 1) * P], bank[0:H, g * P:(g + 1) * P],
                                             ACT.Identity, bias=m.gbias[:, g:g + 1])
                    ring.drained(ins)

        @block.vector
        def _(dve):
            link = Chain(dve, dch)
            dve.wait_ge(e_cc, 1)
            link(dve.tensor_scalar(cct[:, :, :], cct[:, :, :], 1.0, None, ALU.add))
            link(dve.reciprocal(cct[:, :, :], cct[:, :, :]))
            dve.tensor_tensor(ccs[:, :, :].rearrange("p k s -> p s k"), m.cc[:, :, :], cct[:, :, :], ALU.mult).then_inc(silu_c, 1)

            def position(t):
                dve.wait_ge(s_x[t], 16 if t == 0 else 32)
                if t == 0:
                    dve.memset(rs[:, :], 0.0).then_inc(x_pos, 1)
                    return
                if t == 1:
                    dve.wait_ge(s_posc, 32)
                link(dve.tensor_tensor(x[t][:, 0:512], x[t][:, 0:512], posr[t % PS][:, :], ALU.add))
                dve.tensor_tensor(x[t][:, 512:1024], x[t][:, 512:1024], m.posc[:, :], ALU.add).then_inc(x_pos, 1)

            def norm(t):
                s = min(t, 1)
                if t >= 2:
                    dve.wait_ge(full, jobs_before["turn", t - 2] + 2)
                link(dve.scalar_tensor_tensor(hn[t % 2][:, :], x[t][:, :], rs[:, t:t + 1], scale[s][:, :], ALU.mult, ALU.mult))
                dve.tensor_tensor(hn[t % 2][:, :], hn[t % 2][:, :], shift[s][:, :], ALU.add).then_inc(x_hn, 1)

            for kind, t in seq:
                if kind == "mod":
                    for tt in TAKE.get(t, []):
                        position(tt)
                    dve.wait_ge(s_bada[t % 2], 16 * (t // 2 + 1))
                    dve.wait_ge(free, jobs_before["mod", t] + 1)
                    dve.tensor_tensor(mrow[t % 2][:, :], mrow[t % 2][:, :], bada[t % 2][:, :], ALU.add).then_inc(mod_row, 1)
                elif kind == "turn":
                    if t == 0:
                        dve.wait_ge(m.ld, m.ld_all)
                        dve.wait_ge(s_modld, 64)
                        for j in range(2):
                            link(dve.scalar_tensor_tensor(scale[j][:, :], scale[j][:, :], 1.0, m.n1row[:, :], ALU.add, ALU.mult))
                        dve.wait_ge(x_pos, NT)
                        dve.wait_ge(x_sq, NT)
                        link(dve.tensor_scalar(ss[:, :], ss[:, :], 1.0 / D, EPS, ALU.mult, ALU.add))
                        newton_rsqrt(link, dve, ss[:, :], rs[:, :], rt[:, :], ri[:, :])
                        norm(0)
                    if t + 1 < NT:
                        norm(t + 1)


def stage_rglru(nc, a, o, m):
    with ExitStack() as ctx:
        sb = lambda name, shape, dt=F32: ctx.enter_context(nc.sbuf_tensor(name, shape, dt))
        sem = lambda name: ctx.enter_context(nc.semaphore(name))
        NWG = 2
        wg = [sb(f"wg2_{j}", [P, KT, 256]) for j in range(NWG)]
        bd = sb("bd", [P, RT, 2, 2, P])
        xrp = sb("xrp", [P, N + 6])
        xc, tr, ti, aa, sq, hb = (sb(f"rg_{n}", [P, N]) for n in ("xc", "tr", "ti", "aa", "sq", "hb"))
        rows = sb("rows", [P, 2, N])
        mx = sb("mx", [H, 2, N])
        bb = sb("bb", [H, 2, N])
        tmp = [sb(f"rg_t{j}", [P, 512]) for j in range(2)]
        gt = [tr, ti]
        fin = sb("rgfin", [P, 2, RT])
        hlam, lz, lp, lq = (sb(f"lam_{n}", [P, 8]) for n in ("h", "z", "p", "q"))
        hb_g = sb("half_bias", [P, 2, 2, RT])
        mp, ml, dec = (sb(f"row_{n}", [H, 2, NT]) for n in ("mp", "ml", "dec"))
        decd = sb("decd", [H, H, 2, NT])
        mfin = sb("mfin", [H, 2])
        PB = m.banks[2:]
        full, free = sem("full2"), sem("free2")
        dch, ach, pch = sem("dve_chain2"), sem("act_chain2"), sem("pool_chain2")
        s_win = [sem(f"ld_win2_{j}") for j in range(NWG)]
        s_rgw, s_out = sem("ld_rgw"), sem("st_rg")
        zeroed, win_used = sem("zeroed"), sem("win_used2")
        row_d, row_a = sem("rows_dve"), sem("rows_act")
        lam_a, lam_d = sem("lam_exp"), sem("lam_ready")
        conv, xr_in = sem("conv_done"), sem("xr_in")
        gates, q2, root, dir_done = sem("gates_done"), sem("q2_done"), sem("root_done"), sem("dir_done")
        sq_done, sq_used, rs_d = (sem(n) for n in ("sq_done", "sq_used", "rs_d"))
        gelu_sq, gelu_in, gelu_a, gelu_out = (sem(n) for n in ("gelu_squared", "gelu_in", "gelu_tanh", "gelu_out"))
        groups = [XC, XC + 256, RC, RC + 256]
        w_in = a["w_in"][0].rearrange("(k p) n -> p k n", p=P)
        starts = [0, NCTX + 3]

        block = ctx.enter_context(nc.Block())
        NJ_TILE = 3 + 12

        @block.sync
        def _(sp):
            for g in range(4):
                if g >= NWG:
                    sp.wait_ge(win_used, g - NWG + 1)
                sp.dma_start(wg[g % NWG][:, :, :], w_in[:, :, groups[g]:groups[g] + 256]).then_inc(s_win[g % NWG], 16)
                if g == 0:
                    sp.wait_ge(zeroed, 1)
                    for d in range(2):
                        for k, w in enumerate((a["rg_wa"], a["rg_wx"])):
                            for b in range(2):
                                sp.dma_start(bd[64 * b:64 * b + 64, :, d, k, 64 * b:64 * b + 64],
                                             w[0, d].rearrange("(i b) k n -> b k i n", b=2)[b]).then_inc(s_rgw, 16)
            sp.wait_ge(row_d, 4)
            sp.dma_start(o[4][0, 0].rearrange("d h -> h d"), mfin[:, :], allow_slow_non_contiguous=True).then_inc(s_out, 16)
            sp.wait_ge(dir_done, 2 * RT)
            for d in range(2):
                sp.dma_start(feat(o[5][0, 0, d]), fin[:, d, :], allow_slow_non_contiguous=True).then_inc(s_out, 16)
            sp.wait_ge(s_out, 48)

        @block.gpsimd
        def _(pool):
            pool.memset(bd[:, :, :, :, :], 0.0).then_inc(zeroed, 1)
            pool.memset(xrp[:, :], 0.0).then_inc(zeroed, 1)
            pool.memset(rows[:, :, :], 0.0).then_inc(zeroed, 1)

        @block.tensor
        def _(pe):
            ring = Ring(pe, m.ring, full, free)

            def project(g, c0):
                for t0, nt in SPANS:
                    bank = ring.fill()
                    for k in range(KT):
                        mm = pe.matmul(bank[:, 0:nt], wg[g % NWG][:, k, c0:c0 + P], m.hnT[:, k, t0:t0 + nt],
                                       start=(k == 0), stop=(k == KT - 1))
                    ring.filled(mm)

            def xr(i):
                pe.wait_ge(s_win[(i // 2) % NWG], 16)
                if i % 2 == 0:
                    pe.wait_ge(s_win[(i // 2) % NWG], 16)
                project(i // 2, (i % 2) * P)
                if i % 2:
                    pe.wait_ge(full, ring.n)
                    pe.sem_inc(win_used, 1)

            def gr(i):
                g = 2 + i // 2
                pe.wait_ge(s_win[g % NWG], 32)
                project(g, (i % 2) * P)

            pe.wait_ge(s_rgw, 16 * 8)
            xr(0)
            for i in range(RT):
                for d in range(2):
                    for k in range(2):
                        if d == 0 and k == 0:
                            pe.wait_ge(conv, i + 1)
                        for t0, nt in SPANS:
                            bank = ring.fill()
                            ring.filled(pe.matmul(bank[:, 0:nt], bd[:, i, d, k, :], xc[:, t0:t0 + nt], start=True, stop=True))
                    if d == 0 and i + 1 < RT:
                        xr(i + 1)
                if i == 1:
                    pe.wait_ge(row_a, 5)
                    pe.wait_ge(row_d, 6)
                    for j in range(2 * NT):
                        bank = ring.fill()
                        ring.filled(pe.transpose(bank[:, 0:P], rows[:, j // NT, (j % NT) * P:(j % NT + 1) * P], m.ident))
                    bank = ring.fill()
                    ring.filled(pe.matmul(bank[:, 0:H * 2 * NT], m.ones[0:H, :], decd[:, :, :, :].rearrange("p h d c -> p (h d c)"),
                                          start=True, stop=True))
                if i >= 1:
                    gr(i - 1)
            nsq = 0
            for t0, nt in SPANS:
                bank = ring.fill()
                for i in range(RT):
                    nsq += 1
                    pe.wait_ge(sq_done, nsq)
                    mm = pe.matmul(bank[:, 0:nt], m.ones, tmp[i % 2][:, 0:nt], start=(i == 0), stop=(i == RT - 1))
                    if i < RT - 1:
                        mm.then_inc(sq_used, 1)
                ring.filled(mm)
            gr(RT - 1)

        @block.scalar
        def _(act):
            ring = Ring(act, m.ring, full, free)
            link = Chain(act, ach)
            rowj = [0]
            act.wait_ge(lam_d, 1)
            act.activation(lz[:, :], lq[:, :], ACT.Exp, scale=-1.0).then_inc(lam_a, 1)

            def xr(i):
                if i >= 1:
                    act.wait_ge(conv, i)
                else:
                    act.wait_ge(zeroed, 2)
                for t0, nt in SPANS:
                    bank = ring.drain()
                    s = 0 if t0 < NCTX else 1
                    at = starts[s] + 2 + (t0 - SEGS[s][0])
                    ring.drained(act.activation(xrp[:, at:at + nt], bank[:, 0:nt], ACT.Copy))

            def gr(i):
                for t0, nt in SPANS:
                    bank = ring.drain()
                    ring.drained(act.activation(m.yT[:, i, t0:t0 + nt], bank[:, 0:nt], ACT.Copy))

            xr(0)
            act.wait_ge(row_d, 1)
            act.activation(bb[:, :, :], bb[:, :, :], ACT.Exp, scale=-1.0).then_inc(row_a, 1)
            act.wait_ge(row_a, 1)
            act.activation(bb[:, :, :], bb[:, :, :], ACT.Ln, bias=1.0).then_inc(row_a, 1)
            for i in range(RT):
                for d in range(2):
                    for k in range(2):
                        if k == 0 and (i or d):
                            act.wait_ge(dir_done, 2 * i + d)
                        for t0, nt in SPANS:
                            bank = ring.drain()
                            dst = (tr, ti)[k]
                            ring.drained(act.activation(dst[:, t0:t0 + nt], bank[:, 0:nt], ACT.Tanh, scale=0.5,
                                                        bias=hb_g[:, k, d, i:i + 1]))
                    act.wait_ge(free, ring.n)
                    hl = hlam[:, d * RT + i:d * RT + i + 1]
                    link(act.activation(aa[:, :], tr[:, :], ACT.Exp, scale=hl, bias=hl))
                    act.activation(tr[:, :], tr[:, :], ACT.Tanh, scale=hl, bias=hl).then_inc(gates, 1)
                    if d == 0 and i + 1 < RT:
                        xr(i + 1)
                    act.wait_ge(q2, 2 * i + d + 1)
                    act.activation(sq[:, :], sq[:, :], ACT.Sqrt).then_inc(root, 1)
                if i == 0:
                    act.wait_ge(row_d, 5)
                    act.activation(rows[32:32 + H, :, :], rows[32:32 + H, :, :], ACT.Exp)
                    act.activation(rows[64:64 + H, :, :], rows[64:64 + H, :, :], ACT.Exp)
                    act.activation(rows[96:96 + H, :, :], mx[:, :, :], ACT.Exp, scale=-1.0).then_inc(row_a, 1)
                    act.activation(dec[:, :, :], dec[:, :, :], ACT.Exp).then_inc(row_a, 2)
                if i == 1:
                    for j in range(2 * NT):
                        bank = ring.drain()
                        ring.drained(act.activation(m.cols[:, j, :, :], bank[:, 0:P].rearrange("p (q x) -> p q x", x=32)[:, :, 0:H], ACT.Copy))
                    bank = ring.drain()
                    ring.drained(act.activation(m.decb[:, :, :, :].rearrange("p h d c -> p (h d c)"), bank[:, 0:H * 2 * NT], ACT.Copy))
                if i >= 1:
                    gr(i - 1)
            act.wait_ge(dir_done, 2 * RT)
            nsq = 0
            for t0, nt in SPANS:
                for i in range(RT):
                    if nsq >= 2:
                        j, r = divmod(nsq - 2, RT)
                        if r < RT - 1:
                            act.wait_ge(sq_used, j * (RT - 1) + r + 1)
                        else:
                            act.wait_ge(full, ring.n)
                    act.activation(tmp[i % 2][:, 0:nt], m.yT[:, H + i, t0:t0 + nt], ACT.Square).then_inc(sq_done, 1)
                    nsq += 1
                bank = ring.drain()
                ring.drained(act.activation(aa[:, t0:t0 + nt], bank[:, 0:nt], ACT.Identity, scale=1.0 / DRG, bias=m.epsc))
            gr(RT - 1)
            act.wait_ge(rs_d, 1)
            act.activation(aa[:, :], aa[:, :], ACT.Sqrt).then_inc(rs_d, 1)
            act.wait_ge(free, ring.n)

            def square(i):
                if i >= 2:
                    act.wait_ge(gelu_out, i - 1)
                act.activation(gt[i % 2][:, :], m.yT[:, i, :], ACT.Square).then_inc(gelu_sq, 1)

            square(0)
            for i in range(RT):
                if i + 1 < RT:
                    square(i + 1)
                act.wait_ge(gelu_in, i + 1)
                act.activation(gt[i % 2][:, :], gt[i % 2][:, :], ACT.Tanh, scale=0.7978845608028654).then_inc(gelu_a, 1)

        @block.vector
        def _(dve):
            link = Chain(dve, dch)
            link(dve.tensor_scalar(hb_g[:, :, :, :], m.bgate[:, :, :, :], 0.5, None, ALU.mult))
            dve.scalar_tensor_tensor(lq[:, :], m.lam[:, :], -1.0, m.lam[:, :], ALU.mult, ALU.max).then_inc(lam_d, 1)
            dve.wait_ge(lam_a, 1)
            link(dve.tensor_scalar(lp[:, :], lz[:, :], 2.0, None, ALU.add))
            link(dve.reciprocal(lp[:, :], lp[:, :]))
            link(dve.tensor_tensor(lz[:, :], lz[:, :], lp[:, :], ALU.mult))
            link(dve.tensor_tensor(lq[:, :], lz[:, :], lz[:, :], ALU.mult))
            link(dve.tensor_scalar(lp[:, :], lq[:, :], 1.0 / 17, None, ALU.mult))
            for odd in (15, 13, 11, 9, 7, 5, 3):
                link(dve.scalar_tensor_tensor(lp[:, :], lp[:, :], 1.0 / odd, lq[:, :], ALU.add, ALU.mult))
            link(dve.scalar_tensor_tensor(lp[:, :], lp[:, :], 1.0, lz[:, :], ALU.add, ALU.mult))
            link(dve.tensor_scalar(lp[:, :], lp[:, :], 2.0, None, ALU.mult))
            link(dve.tensor_scalar(lq[:, :], m.lam[:, :], -1.0, 0.0, ALU.mult, ALU.max))
            link(dve.tensor_tensor(lp[:, :], lp[:, :], lq[:, :], ALU.add))
            link(dve.tensor_scalar(hlam[:, :], lp[:, :], -4.0, None, ALU.mult))

            ig, fg = m.g4[:, 0:4:2, :], m.g4[:, 1:4:2, :]
            dve.scalar_tensor_tensor(bb[:, :, :], fg, -1.0, fg, ALU.mult, ALU.max).then_inc(row_d, 1)

            def conv_tile(i):
                dve.wait_ge(free, NJ_TILE * i + 3 - (6 if i else 0) + (extra(i)))
                for s, (t0, nt) in enumerate(SEGS):
                    for j in range(4):
                        src = xrp[:, starts[s] + j:starts[s] + j + nt]
                        wj = m.convw[:, j, i:i + 1]
                        if j == 0:
                            ins = dve.tensor_scalar(xc[:, t0:t0 + nt], src, wj, m.convb[:, i:i + 1], ALU.mult, ALU.add)
                        else:
                            ins = dve.scalar_tensor_tensor(xc[:, t0:t0 + nt], src, wj, xc[:, t0:t0 + nt], ALU.mult, ALU.add)
                        if s == 1 and j == 3:
                            ins.then_inc(conv, 1)
                            dve.wait_ge(conv, i + 1)
                        else:
                            link(ins)

            def extra(i):
                return 2 * NT + 1 + 3 if i >= 3 else 0

            def flip(ap, d):
                return ap[:, ::-1] if d else ap

            def rg_dir(i, d):
                n = 2 * i + d
                dve.wait_ge(gates, n + 1)
                link(dve.tensor_tensor(sq[:, :], aa[:, :], aa[:, :], ALU.mult))
                link(dve.tensor_scalar(sq[:, :], sq[:, :], -0.25, -0.25, ALU.mult, ALU.add))
                dve.tensor_tensor(sq[:, :], tr[:, :], sq[:, :], ALU.mult).then_inc(q2, 1)
                link(dve.scalar_tensor_tensor(ti[:, :], ti[:, :], 1.0, xc[:, :], ALU.add, ALU.mult))
                dve.wait_ge(root, n + 1)
                link(dve.tensor_tensor(ti[:, :], ti[:, :], sq[:, :], ALU.mult))
                y = m.yT[:, H + i, :]
                dst = hb[:, :] if d else y
                link(dve.tensor_tensor_scan(flip(dst[:, 0:NCTX], d), flip(aa[:, 0:NCTX], d), flip(ti[:, 0:NCTX], d),
                                            0.0, ALU.mult, ALU.add))
                link(dve.tensor_tensor_scan(flip(dst[:, NCTX:N], d), flip(aa[:, NCTX:N], d), flip(ti[:, NCTX:N], d),
                                            m.h0c[:, d, i:i + 1], ALU.mult, ALU.add))
                last = dst[:, 0:1] if d else dst[:, NCTX - 1:NCTX]
                ins = dve.tensor_copy(fin[:, d, i:i + 1], last)
                if d:
                    link(ins)
                    ins = dve.tensor_tensor(y, y, hb[:, :], ALU.add)
                ins.then_inc(dir_done, 1)
                dve.wait_ge(dir_done, n + 1)

            conv_tile(0)
            dve.wait_ge(row_a, 2)
            link(dve.scalar_tensor_tensor(bb[:, :, :], fg, 0.0, bb[:, :, :], ALU.min, ALU.subtract))
            for d in range(2):
                for s, (t0, nt) in enumerate(SEGS):
                    link(dve.tensor_tensor_scan(flip(mx[:, d, t0:t0 + nt], d), flip(bb[:, d, t0:t0 + nt], d),
                                                flip(m.g4[:, 2 * d, t0:t0 + nt], d),
                                                m.m0[:, d:d + 1] if s else 0.0, ALU.add, ALU.max))
            link(dve.tensor_copy(mfin[:, 0:1], mx[:, 0, NCTX - 1:NCTX]))
            dve.tensor_copy(mfin[:, 1:2], mx[:, 1, 0:1]).then_inc(row_d, 3)
            link(dve.memset(mp[:, :, 0:1], 0.0))
            link(dve.tensor_copy(mp[:, 0, 1:2], m.m0[:, 0:1]))
            link(dve.tensor_copy(mp[:, 1, NT - 1:NT], m.m0[:, 1:2]))
            link(dve.tensor_copy(mp[:, 0, 2:NT], mx[:, 0, 2 * P - 1:N - P:P]))
            link(dve.tensor_copy(mp[:, 1, 1:NT - 1], mx[:, 1, 2 * P:N:P]))
            rg_dir(0, 0)
            for d in range(2):
                for c in range(NT):
                    ch = flip(bb[:, d, c * P:(c + 1) * P], d)
                    link(dve.tensor_tensor_scan(ch, m.ones[0:H, :], ch, 0.0, ALU.mult, ALU.add))
            link(dve.tensor_tensor(m.mn, bb[:, :, :], mx[:, :, :], ALU.subtract))
            dve.wait_ge(zeroed, 3)
            link(dve.tensor_tensor(rows[0:H, :, :], ig, bb[:, :, :], ALU.subtract))
            link(dve.tensor_copy(ml[:, 0, :], m.mn[:, 0, P - 1:N:P]))
            link(dve.tensor_copy(ml[:, 1, :], m.mn[:, 1, 0:N:P]))
            ch4 = lambda ap: ap.rearrange("p d (c t) -> p d c t", t=P)
            spread = lambda ap: ap.unsqueeze(3).to_broadcast([H, 2, NT, P])
            link(dve.tensor_tensor(ch4(rows[32:32 + H, :, :]), ch4(rows[0:H, :, :]), spread(ml[:, :, :]), ALU.add))
            link(dve.tensor_tensor(ch4(rows[64:64 + H, :, :]), ch4(m.mn), spread(mp[:, :, :]), ALU.add))
            dve.tensor_tensor(dec[:, :, :], mp[:, :, :], ml[:, :, :], ALU.add).then_inc(row_d, 1)
            rg_dir(0, 1)
            conv_tile(1)
            rg_dir(1, 0)
            dve.wait_ge(row_a, 5)
            for h in range(H):
                ins = dve.tensor_scalar(decd[:, h, :, :], dec[:, :, :], m.cst[0:H, C_ID + h:C_ID + h + 1], None, ALU.mult)
            ins.then_inc(row_d, 1)
            rg_dir(1, 1)
            for i in (2, 3):
                conv_tile(i)
                rg_dir(i, 0)
                rg_dir(i, 1)
            rg_jobs = 3 * RT + 12 * RT + 2 * NT + 1 + 3 * (RT - 1)
            dve.wait_ge(free, rg_jobs + 3)
            dve.reciprocal(aa[:, :], aa[:, :]).then_inc(rs_d, 1)
            dve.wait_ge(rs_d, 2)

            def cubic(i):
                y, u, t = m.yT[:, H + i, :], m.yT[:, i, :], gt[i % 2]
                link(dve.scalar_tensor_tensor(y, y, m.rgnc[:, i:i + 1], aa[:, :], ALU.mult, ALU.mult))
                dve.wait_ge(gelu_sq, i + 1)
                link(dve.tensor_scalar(t[:, :], t[:, :], 0.044715, 1.0, ALU.mult, ALU.add))
                dve.tensor_tensor(t[:, :], t[:, :], u, ALU.mult).then_inc(gelu_in, 1)

            cubic(0)
            for i in range(RT):
                if i == 0:
                    cubic(1)
                y, u, t = m.yT[:, H + i, :], m.yT[:, i, :], gt[i % 2]
                dve.wait_ge(gelu_a, i + 1)
                link(dve.scalar_tensor_tensor(t[:, :], t[:, :], 1.0, u, ALU.add, ALU.mult))
                dve.scalar_tensor_tensor(y, t[:, :], 0.5, y, ALU.mult, ALU.mult).then_inc(gelu_out, 1)
                if i + 2 < RT:
                    cubic(i + 2)


def stage_mlstm(nc, a, o, m):
    with ExitStack() as ctx:
        sb = lambda name, shape, dt=F32: ctx.enter_context(nc.sbuf_tensor(name, shape, dt))
        sem = lambda name: ctx.enter_context(nc.semaphore(name))
        NW = 3
        wg = [sb(f"wg3_{j}", [P, KT, 256]) for j in range(NW)]
        qT, kT = sb("qT", [P, H, N]), sb("kT", [P, H, N])
        v = sb("v", [P, NT, H, P + 1])
        hbuf = sb("hbuf", [P, NT, H, P])
        S = sb("S", [P, 2, 2, H, P + 1])
        eb = [sb(f"eb{j}", [P, H, P]) for j in range(2)]
        kw = sb("kw", [P, H, P])
        ob = sb("ob", [P, H, P])
        sqs = sb("sqs", [P, P])
        nd = sb("nd", [P, H, P + 1])
        d1, ss, rs, rt = (sb(f"ml_{n}", [P, H]) for n in ("den", "ss", "rs", "rt"))
        ri = sb("ml_ri", [P, H], I32)
        PS, PM, PX = m.banks[2], m.banks[3], m.banks[4:8]
        full, free = sem("full3"), sem("free3")
        dch = sem("dve_chain3")
        s_w = [sem(f"ld_win3_{j}") for j in range(NW)]
        w_used, s_state, s_out, pset = sem("win_used3"), sem("ld_state"), sem("st_state"), sem("ones_set")
        logw_in, logw, weights, probs, keys, products, unit_done = (sem(n) for n in (
            "scores_ready", "logw_ready", "weights_ready", "probs_ready", "keys_ready", "products_ready", "unit_done"))
        h_new, fin_sq, y_ready = sem("h_new"), sem("fin_squares"), sem("y_ready")
        w_in = a["w_in"][0].rearrange("(k p) n -> p k n", p=P)
        groups = [QC, QC + 256, KC, KC + 256, VC, VC + 256, OC, OC + 256]

        order = [(0, 0), (1, 0)]
        for j in range(1, NT):
            order += [(0, j), (1, NT - j)]
        met, units = set(), []
        for d, c in order:
            units.append((d, c, c in met))
            met.add(c)
        U = len(units)

        def px(j):
            return PX[j // 3][:, (j % 3) * (P + 1):(j % 3 + 1) * (P + 1)]

        block = ctx.enter_context(nc.Block())

        @block.sync
        def _(sp):
            for g, c0 in enumerate(groups):
                if g >= NW:
                    sp.wait_ge(w_used, g - NW + 1)
                sp.dma_start(wg[g % NW][:, :, :], w_in[:, :, c0:c0 + 256]).then_inc(s_w[g % NW], 16)
                if g == 3:
                    for d in range(2):
                        sp.dma_start(S[:, 1, d, :, 0:P], a["state_mlstm_C"][0, 0, d].rearrange("h d e -> d h e")).then_inc(s_state, 16)
                        sp.dma_start(S[:, 1, d, :, P:P + 1], a["state_mlstm_n"][0, 0, d].rearrange("h (d o) -> d h o", o=1),
                                     allow_slow_non_contiguous=True).then_inc(s_state, 16)
            sp.wait_ge(unit_done, 2)
            for d in range(2):
                sp.dma_start(o[2][0, 0, d].rearrange("h d e -> d h e"), S[:, 0, d, :, 0:P]).then_inc(s_out, 16)
                sp.dma_start(o[3][0, 0, d].rearrange("h (d o) -> d h o", o=1), S[:, 0, d, :, P:P + 1],
                             allow_slow_non_contiguous=True).then_inc(s_out, 16)
            sp.wait_ge(s_out, 64)

        @block.gpsimd
        def _(pool):
            pool.memset(v[:, :, :, P:P + 1], 1.0).then_inc(pset, 1)
            pool.memset(S[:, 0, :, :, :], 0.0).then_inc(pset, 1)

        @block.tensor
        def _(pe):
            ring = Ring(pe, m.ring, full, free)

            def used():
                pe.wait_ge(full, ring.n)
                pe.sem_inc(w_used, 1)

            for mt in range(2 * H):
                g = mt // 2
                if mt % 2 == 0:
                    pe.wait_ge(s_w[g % NW], 16 * (g // NW + 1))
                for t0, nt in SPANS:
                    bank = ring.fill()
                    for k in range(KT):
                        mm = pe.matmul(bank[:, 0:nt], wg[g % NW][:, k, (mt % 2) * P:(mt % 2 + 1) * P], m.hnT[:, k, t0:t0 + nt],
                                       start=(k == 0), stop=(k == KT - 1))
                    ring.filled(mm)
                if mt % 2:
                    used()

            def token_major(g, t):
                bank = ring.fill()
                for j in range(2):
                    for k in range(KT):
                        mm = pe.matmul(bank[:, j * 256:(j + 1) * 256], m.hnT[:, k, t * P:(t + 1) * P],
                                       wg[(g + j) % NW][:, k, :], start=(k == 0), stop=(k == KT - 1))
                ring.filled(mm)

            pe.wait_ge(s_w[4 % NW], 32)
            pe.wait_ge(s_w[5 % NW], 32)
            for t in range(NT):
                token_major(4, t)
            used()
            used()
            pe.wait_ge(free, ring.n)
            pe.wait_ge(pset, 2)
            pe.wait_ge(s_state, 64)
            for n in range(-1, U + 1):
                if n + 1 < U:
                    d, c, _ = units[n + 1]
                    ch = slice(c * P, (c + 1) * P)
                    if n >= 0:
                        pe.wait_ge(probs, n + 1)
                    for h in range(H):
                        pe.matmul(PM[:, h * P:(h + 1) * P], m.sel[:, h, :], m.mn[:, d, ch], start=True, stop=True)
                    for h in range(H):
                        mm = pe.matmul(PS[:, h * P:(h + 1) * P], kT[:, h, ch], qT[:, h, ch], start=True, stop=True)
                    mm.then_inc(logw_in, 1)
                    bank = ring.fill()
                    for h in range(H):
                        mm = pe.transpose(bank[:, h * P:(h + 1) * P], kT[:, h, ch], m.ident)
                    ring.filled(mm)
                if 0 <= n < U:
                    d, c, second = units[n]
                    seq = min(c, 1)
                    if second:
                        if n == [j for j in range(U) if units[j][2]][0]:
                            pe.wait_ge(s_w[6 % NW], 48)
                            pe.wait_ge(s_w[7 % NW], 48)
                        token_major(6, c)
                    if n >= 1:
                        pe.wait_ge(unit_done, n)
                    for h in range(H):
                        pe.matmul(px(4 + h), qT[:, h, c * P:(c + 1) * P], S[:, seq, d, h, :], start=True, stop=True)
                    pe.wait_ge(probs, n + 1)
                    for h in range(H):
                        pe.matmul(px(h), eb[n % 2][:, h, :], v[:, c, h, :], start=True, stop=True)
                    pe.wait_ge(keys, n + 1)
                    for h in range(H):
                        mm = pe.matmul(px(8 + h), kw[:, h, :], v[:, c, h, :], start=True, stop=True)
                    mm.then_inc(products, 1)
                if n >= 1 and units[n - 1][2]:
                    bank = ring.fill()
                    pe.wait_ge(y_ready, sum(u[2] for u in units[:n]))
                    for h in range(H):
                        mm = pe.transpose(bank[:, h * P:(h + 1) * P], hbuf[:, units[n - 1][1], h, :], m.ident)
                    ring.filled(mm)

        @block.scalar
        def _(act):
            ring = Ring(act, m.ring, full, free)
            for mt in range(2 * H):
                dst, scale = ((qT, 1.0), (kT, float(P) ** -0.5))[mt // H]
                for t0, nt in SPANS:
                    bank = ring.drain()
                    ring.drained(act.activation(dst[:, mt % H, t0:t0 + nt], bank[:, 0:nt], ACT.Copy, scale=scale))
            for t in range(NT):
                bank = ring.drain()
                ring.drained(act.activation(v[:, t, :, 0:P], bank[:, :].rearrange("p (h e) -> p h e", h=H), ACT.Copy))
            for n in range(-1, U + 1):
                fins = sum(u[2] for u in units[:max(n, 0)])
                if n + 1 < U:
                    d, c, _ = units[n + 1]
                    j = d * NT + c
                    act.wait_ge(logw, n + 2)
                    act.activation(eb[(n + 1) % 2][:, :, :], eb[(n + 1) % 2][:, :, :], ACT.Exp).then_inc(weights, 1)
                    bank = ring.drain()
                    if n >= 0:
                        act.wait_ge(products, n + 1)
                    for h in range(H):
                        ins = act.activation(kw[:, h, :], bank[:, h * P:(h + 1) * P], ACT.Copy, scale=m.cols[:, j, 1, h:h + 1])
                    ring.drained(ins)
                    act.wait_ge(free, ring.n)
                    act.sem_inc(keys, 1)
                if 0 <= n < U and units[n][2]:
                    bank = ring.drain()
                    if fins >= 1:
                        act.wait_ge(y_ready, fins)
                    ring.drained(act.activation(ob[:, :, :], bank[:, :].rearrange("p (h e) -> p h e", h=H), ACT.Tanh, scale=0.5))
                if n >= 1 and units[n - 1][2]:
                    c = units[n - 1][1]
                    bank = ring.drain()
                    for h in range(H):
                        ins = act.activation(m.yT[:, h, c * P:(c + 1) * P], bank[:, h * P:(h + 1) * P], ACT.Copy,
                                             scale=m.mlnc[:, h:h + 1])
                    ring.drained(ins)
                if 0 <= n < U and units[n][2]:
                    c = units[n][1]
                    act.wait_ge(h_new, n + 1)
                    if fins >= 1:
                        act.wait_ge(y_ready, fins)
                    for h in range(H):
                        ins = act.activation(sqs[:, :], hbuf[:, c, h, :], ACT.Square, accum_out=ss[:, h:h + 1])
                        ins.then_inc(fin_sq, 1)
                        act.wait_ge(fin_sq, H * fins + h + 1)

        @block.vector
        def _(dve):
            link = Chain(dve, dch)
            fins = 0
            first = 3 * 2 * H + NT
            for n in range(-1, U + 1):
                if n + 1 < U:
                    d, c, _ = units[n + 1]
                    j = d * NT + c
                    dve.wait_ge(logw_in, n + 2)
                    if n >= 1:
                        dve.wait_ge(products, n)
                    for h in range(H):
                        ins = dve.scalar_tensor_tensor(eb[(n + 1) % 2][:, h, :], PM[:, h * P:(h + 1) * P],
                                                       m.cols[:, j, 0, h:h + 1], m.neg[d], ALU.add, ALU.add)
                    ins.then_inc(logw, 1)
                if 0 <= n < U:
                    d, c, second = units[n]
                    seq, j = min(c, 1), d * NT + c
                    dve.wait_ge(products, n + 1)
                    for h in range(H):
                        ins = dve.tensor_scalar(nd[:, h, :], px(4 + h), m.cols[:, j, 2, h:h + 1], None, ALU.mult)
                    link(ins)
                    for h in range(H):
                        ins = dve.tensor_tensor(nd[:, h, :], nd[:, h, :], px(h), ALU.add)
                    link(ins)
                    for h in range(H):
                        st = S[:, seq, d, h, :]
                        ins = dve.scalar_tensor_tensor(st, st, m.decb[:, h, d, c:c + 1], px(8 + h), ALU.mult, ALU.add)
                    ins.then_inc(unit_done, 1)
                    dve.wait_ge(unit_done, n + 1)
                if n + 1 < U:
                    dve.wait_ge(weights, n + 2)
                    e = eb[(n + 1) % 2]
                    dve.tensor_tensor(e[:, :, :], e[:, :, :], PS[:, :].rearrange("p (h t) -> p h t", h=H), ALU.mult).then_inc(probs, 1)
                if 0 <= n < U:
                    dn = nd[:, :, P]
                    link(dve.scalar_tensor_tensor(d1[:, :], dn, -1.0, dn, ALU.mult, ALU.max))
                    link(dve.tensor_tensor(d1[:, :], d1[:, :], m.cols[:, j, 3, :], ALU.max))
                    link(dve.reciprocal(d1[:, :], d1[:, :]))
                    rd = d1[:, :].unsqueeze(2).to_broadcast([P, H, P])
                    if second:
                        link(dve.tensor_tensor(nd[:, :, 0:P], nd[:, :, 0:P], rd, ALU.mult))
                        link(dve.tensor_tensor(hbuf[:, c, :, :], hbuf[:, c, :, :], nd[:, :, 0:P], ALU.add))
                    else:
                        link(dve.tensor_tensor(hbuf[:, c, :, :], nd[:, :, 0:P], rd, ALU.mult))
                    dve.sem_inc(h_new, 1)
                if 0 <= n < U and units[n][2]:
                    c = units[n][1]
                    fins += 1
                    dve.wait_ge(fin_sq, H * fins)
                    link(dve.tensor_scalar(ss[:, :], ss[:, :], 1.0 / P, EPS, ALU.mult, ALU.add))
                    newton_rsqrt(link, dve, ss[:, :], rs[:, :], rt[:, :], ri[:, :])
                    link(dve.tensor_scalar(rs[:, :], rs[:, :], 0.5, None, ALU.mult))
                    hb = hbuf[:, c, :, :]
                    jobs = first + (min(n + 2, U)) + sum(u[2] for u in units[:n + 1]) + sum(u[2] for u in units[:max(n - 1, 0)])
                    dve.wait_ge(free, jobs)
                    link(dve.scalar_tensor_tensor(hb, ob[:, :, :], 1.0, hb, ALU.add, ALU.mult))
                    dve.tensor_tensor(hb, hb, rs[:, :].unsqueeze(2).to_broadcast([P, H, P]), ALU.mult).then_inc(y_ready, 1)
                    dve.wait_ge(y_ready, fins)

def stage_route(nc, a, m):
    with ExitStack() as ctx:
        sb = lambda name, shape, dt=F32: ctx.enter_context(nc.sbuf_tensor(name, shape, dt))
        sem = lambda name: ctx.enter_context(nc.semaphore(name))
        wo = sb("wo", [P, KT, D])
        gate, scale, shift = ([sb(f"{n}2_{s}", [P, D]) for s in range(2)] for n in ("gate", "scale", "shift"))
        n2row = sb("n2row", [P, D])
        x = [sb(f"x2_{j}", [P, D]) for j in range(2)]
        hn = [sb(f"hn2_{j}", [P, D]) for j in range(2)]
        sq = sb("sq4", [P, D])
        hT = [sb(f"hT4_{j}", [P, KT, P]) for j in range(2)]
        rw, rbias = sb("rw", [P, KT, NE]), sb("rbias", [P, NE])
        ss, rs, rt = sb("ss4", [P, NT]), sb("rs4", [P, 1]), sb("rt4", [P, 1])
        ri = sb("ri4", [P, 1], I32)
        sc, sbias, work, chosen = (sb(f"rt_{n}", [P, NE]) for n in ("sc", "sb", "work", "chosen"))
        ex = [sb(f"rt_ex{j}", [P, NE]) for j in range(2)]
        top = sb("rt_top", [P, NGRP, 8])
        gs, gr = sb("rt_gs", [P, 16]), sb("rt_gr", [P, 16])
        t8 = sb("rt_t8", [P, 8])
        mask = sb("mask", [P, NT, NE])
        maskb = [sb(f"maskb{j}", [P, NE], BF16) for j in range(2)]
        before = [sb(f"before{j}", [P, NE], BF16) for j in range(2)]
        trib, onesb = sb("trib", [P, P], BF16), sb("onesb", [P, P], BF16)
        nb, incl, cnt = sb("nb", [P, NE]), sb("incl", [P, NE]), sb("cnt", [P, NE])
        blk, sh, zero = sb("blk", [P, 2]), sb("sh", [P, 1]), sb("zero", [P, D])
        wsum = sb("wsum", [P, 1])
        full, free = sem("full4"), sem("free4")
        dch = sem("dve_chain4")
        s_wo, s_in, s_x = sem("ld_wo"), sem("ld_route"), [sem(f"ld_x2_{j}") for j in range(2)]
        s_x2, s_hn = [sem(f"st_x2_{j}") for j in range(2)], [sem(f"st_hn2_{j}") for j in range(2)]
        s_zero, zero_set = sem("st_zero"), sem("zero_set")
        mixed, x2_new, x2_sq, hn_new, picked, cnt_in = (sem(n) for n in (
            "mixed", "x2_new", "x2_sq", "hn2_new", "picked", "count_ready"))
        block = ctx.enter_context(nc.Block())

        @block.sync
        def _(sp):
            def load_x(t):
                if t >= 2:
                    sp.wait_ge(hn_new, t - 1)
                    sp.wait_ge(s_x2[t % 2], 16 * (t // 2))
                sp.dma_start(x[t % 2][:, :], m.x1[t * P:(t + 1) * P, :]).then_inc(s_x[t % 2], 16)

            def store(t):
                rows = slice(t * P, (t + 1) * P)
                sp.wait_ge(x2_new, t + 1)
                sp.dma_start(m.x2[rows, :], x[t % 2][:, :]).then_inc(s_x2[t % 2], 16)
                sp.wait_ge(hn_new, t + 1)
                sp.dma_start(m.hn2[rows, :], hn[t % 2][:, :]).then_inc(s_hn[t % 2], 16)

            sp.dma_start(wo[:, :, :], a["w_out"][0].rearrange("(k p) n -> p k n", p=P)).then_inc(s_wo, 16)
            load_x(0)
            n_in = 0
            for s in range(2):
                for dst, part in ((gate, 2), (shift, 3), (scale, 4)):
                    sp.dma_start(dst[s][:, :], m.mods[s:s + 1, part * D:(part + 1) * D].to_broadcast([P, D])).then_inc(s_in, 16)
                    n_in += 1
            sp.dma_start(n2row[:, :], a["norm2"].to_broadcast([P, D])).then_inc(s_in, 16)
            sp.dma_start(rw[:, :, :], a["router_w"][0].rearrange("(k p) n -> p k n", p=P)).then_inc(s_in, 16)
            sp.dma_start(rbias[:, :], a["router_bias"].to_broadcast([P, NE])).then_inc(s_in, 16)
            m.n_route = 16 * (n_in + 3)
            for t in range(1, NT):
                load_x(t)
                store(t - 1)
            store(NT - 1)
            for j in range(2):
                n = (NT + 1 - j) // 2
                sp.wait_ge(s_x2[j], 16 * n)
                sp.wait_ge(s_hn[j], 16 * n)

        @block.gpsimd
        def _(pool):
            pool.memset(zero[:, :], 0.0).then_inc(zero_set, 1)
            pool.wait_ge(zero_set, 1)
            pool.wait_ge(mixed, 2)
            for t in range(ROWS // P):
                pool.dma_start(m.yacc[t * P:(t + 1) * P, :], zero[:, :]).then_inc(s_zero, 16)
            pool.dma_start(m.hn2[N:ROWS, :], zero[:, :]).then_inc(s_zero, 16)
            pool.wait_ge(s_zero, 16 * (ROWS // P + 1))

        @block.tensor
        def _(pe):
            ring = Ring(pe, m.ring, full, free)

            def mix(t):
                if t >= 2:
                    pe.wait_ge(x2_new, t - 1)
                for half in range(2):
                    bank = m.banks[2 + 2 * (t % 2) + half]
                    for k in range(KT):
                        mm = pe.matmul(bank[:, :], m.yT[:, k, t * P:(t + 1) * P], wo[:, k, half * 512:(half + 1) * 512],
                                       start=(k == 0), stop=(k == KT - 1))
                mm.then_inc(mixed, 1)

            def places(t):
                bank = ring.fill()
                pe.wait_ge(picked, t + 1)
                pe.matmul(bank[:, 0:NE], trib[:, :], maskb[t % 2][:, :], start=True, stop=False)
                ring.filled(pe.matmul(bank[:, 0:NE], onesb[:, :], before[t % 2][:, :], start=False, stop=True))

            pe.wait_ge(s_wo, 16)
            mix(0)
            pe.wait_ge(s_in, m.n_route)
            for t in range(NT):
                if t + 1 < NT:
                    mix(t + 1)
                pe.wait_ge(hn_new, t + 1)
                for half in range(2):
                    bank = ring.fill()
                    for k in range(4):
                        kk = 4 * half + k
                        mm = pe.transpose(bank[:, k * P:(k + 1) * P], hn[t % 2][:, kk * P:(kk + 1) * P], m.ident)
                    ring.filled(mm)
                bank = ring.fill()
                pe.wait_ge(free, ring.n)
                for k in range(KT):
                    mm = pe.matmul(bank[:, 0:NE], hT[t % 2][:, k, :], rw[:, k, :], start=(k == 0), stop=(k == KT - 1))
                ring.filled(mm)
                if t >= 1:
                    places(t - 1)
            places(NT - 1)
            bank = ring.fill()
            pe.wait_ge(picked, NT + 1)
            ring.filled(pe.matmul(bank[:, 0:NE], onesb[:, :], before[NT % 2][:, :], start=True, stop=True))
            bank = ring.fill()
            pe.wait_ge(cnt_in, 1)
            for j in range(2):
                mm = pe.transpose(bank[0:1, j * P:(j + 1) * P], blk[:, j:j + 1], m.ident)
            ring.filled(mm)

        @block.scalar
        def _(act):
            ring = Ring(act, m.ring, full, free)

            def place_out(t):
                bank = ring.drain()
                ring.drained(act.activation(m.dest[:, t, 0:NE], bank[:, 0:NE], ACT.Copy))

            for t in range(NT):
                act.wait_ge(x2_new, t + 1)
                if t >= 1:
                    act.wait_ge(x2_sq, t)
                act.activation(sq[:, :], x[t % 2][:, :], ACT.Square, accum_out=ss[:, t:t + 1]).then_inc(x2_sq, 1)
                for half in range(2):
                    bank = ring.drain()
                    ring.drained(act.activation(hT[t % 2][:, 4 * half:4 * half + 4, :],
                                                bank[:, :].rearrange("p (k n) -> p k n", k=4), ACT.Copy))
                bank = ring.drain()
                if t >= 2:
                    act.wait_ge(picked, t - 1)
                ring.drained(act.activation(ex[t % 2][:, :], bank[:, 0:NE], ACT.Exp, scale=-1.0))
                if t >= 1:
                    place_out(t - 1)
            place_out(NT - 1)
            bank = ring.drain()
            ring.drained(act.activation(cnt[:, :], bank[:, 0:NE], ACT.Copy))
            bank = ring.drain()
            ring.drained(act.activation(m.tab[:, 0:2 * P], bank[0:1, 0:2 * P], ACT.Copy))

        @block.vector
        def _(dve):
            link = Chain(dve, dch)
            link(dve.tensor_copy(trib[:, :], m.tri))
            link(dve.tensor_copy(onesb[:, :], m.ones))
            link(dve.memset(before[0][:, :], 0.0))
            link(dve.memset(gs[:, NGRP:16], -BIG))
            link(dve.memset(t8[:, :], -BIG))
            dve.wait_ge(s_in, m.n_route)
            for s in range(2):
                link(dve.scalar_tensor_tensor(scale[s][:, :], scale[s][:, :], 1.0, n2row[:, :], ALU.add, ALU.mult))

            def residual(t):
                s = min(t, 1)
                dve.wait_ge(mixed, t + 1)
                dve.wait_ge(s_x[t % 2], 16 * (t // 2 + 1))
                if t >= 2:
                    dve.wait_ge(s_hn[t % 2], 16 * (t // 2))
                    dve.wait_ge(full, jobs(t - 2) + 2)
                h = hn[t % 2]
                for half in range(2):
                    c = slice(half * 512, (half + 1) * 512)
                    ins = dve.tensor_tensor(h[:, c], m.banks[2 + 2 * (t % 2) + half][:, :], gate[s][:, c], ALU.mult)
                link(ins)
                dve.tensor_tensor(x[t % 2][:, :], x[t % 2][:, :], h[:, :], ALU.add).then_inc(x2_new, 1)
                dve.wait_ge(x2_sq, t + 1)
                v = ss[:, t:t + 1]
                link(dve.tensor_scalar(v, v, 1.0 / D, EPS, ALU.mult, ALU.add))
                newton_rsqrt(link, dve, v, rs[:, :], rt[:, :], ri[:, :])
                link(dve.scalar_tensor_tensor(h[:, :], x[t % 2][:, :], rs[:, :], scale[s][:, :], ALU.mult, ALU.mult))
                dve.tensor_tensor(h[:, :], h[:, :], shift[s][:, :], ALU.add).then_inc(hn_new, 1)
                dve.wait_ge(hn_new, t + 1)

            def jobs(t):
                return 3 * t + max(t - 1, 0)

            def pick(t):
                dve.wait_ge(free, jobs(t) + 3)
                link(dve.tensor_scalar(sc[:, :], ex[t % 2][:, :], 1.0, None, ALU.add))
                link(dve.reciprocal(sc[:, :], sc[:, :]))
                link(dve.tensor_tensor(sbias[:, :], sc[:, :], rbias[:, :], ALU.add))
                for g in range(NGRP):
                    ins = dve.max(top[:, g, :], sbias[:, g * 8:(g + 1) * 8])
                link(ins)
                link(dve.tensor_tensor(gs[:, 0:NGRP], top[:, :, 0], top[:, :, 1], ALU.add))
                link(dve.max(gr[:, 0:8], gs[:, 0:NGRP]))
                link(dve.tensor_copy(t8[:, 0:4], gr[:, 0:4]))
                link(dve.match_replace(gr[:, :], t8[:, :], gs[:, :], BIG))
                link(dve.tensor_scalar(gr[:, 0:8], gr[:, 0:8], BIG, None, ALU.is_equal))
                link(dve.tensor_scalar(gr[:, 8:16], gr[:, 0:8], BIG, -BIG, ALU.mult, ALU.add))
                spread = gr[:, 8:16].unsqueeze(2).to_broadcast([P, NGRP, 8])
                link(dve.tensor_tensor(work[:, :].rearrange("p (g e) -> p g e", g=NGRP),
                                       sbias[:, :].rearrange("p (g e) -> p g e", g=NGRP), spread, ALU.add))
                link(dve.max(gr[:, 0:8], work[:, :]))
                link(dve.match_replace(chosen[:, :], gr[:, 0:8], work[:, :], BIG))
                mk = mask[:, t, :]
                link(dve.tensor_scalar(mk, chosen[:, :], BIG, None, ALU.is_equal))
                link(dve.tensor_tensor(sc[:, :], sc[:, :], mk, ALU.mult))
                link(dve.reduce_sum(wsum[:, :], sc[:, :], AX))
                link(dve.reciprocal(wsum[:, :], wsum[:, :]))
                link(dve.tensor_scalar(sc[:, :], sc[:, :], wsum[:, :], 2.5, ALU.mult, ALU.mult))
                for part in range(3):
                    w = m.w3[:, t, 0:NE, part]
                    link(dve.tensor_copy(w, sc[:, :]))
                    if part < 2:
                        link(dve.tensor_tensor(sc[:, :], sc[:, :], w, ALU.subtract))
                if t >= 1:
                    dve.wait_ge(full, jobs(t) + 4)
                link(dve.tensor_tensor(before[(t + 1) % 2][:, :], before[t % 2][:, :], mk, ALU.add))
                dve.tensor_copy(maskb[t % 2][:, :], mk).then_inc(picked, 1)

            residual(0)
            for t in range(NT):
                if t + 1 < NT:
                    residual(t + 1)
                pick(t)
            dve.tensor_copy(wsum[:, :], m.ones[:, 0:1]).then_inc(picked, 1)
            total = jobs(NT) + 1
            dve.wait_ge(free, total + 1)
            link(dve.tensor_copy(nb[:, :], m.ones[:, 0:NE]))
            for j in range(1, NT):
                link(dve.scalar_tensor_tensor(nb[:, :], cnt[:, :], float(P * j), nb[:, :], ALU.is_gt, ALU.add))
            link(dve.tensor_tensor_scan(incl[:, :], m.ones[:, 0:NE], nb[:, :], 0.0, ALU.mult, ALU.add))
            for j in range(2):
                link(dve.tensor_scalar(work[:, :], incl[:, :], m.cst[:, C_BLK + j:C_BLK + j + 1], None, ALU.is_le))
                link(dve.reduce_sum(blk[:, j:j + 1], work[:, :], AX))
            dve.tensor_copy(wsum[:, :], m.ones[:, 0:1]).then_inc(cnt_in, 1)
            link(dve.tensor_tensor(nb[:, :], incl[:, :], nb[:, :], ALU.subtract))
            link(dve.tensor_scalar(nb[:, :], nb[:, :], float(P), 1.0, ALU.mult, ALU.add))
            ds = m.dest[:, :, 0:NE]
            link(dve.tensor_tensor(ds, ds, nb[:, :].unsqueeze(1).to_broadcast([P, NT, NE]), ALU.add))
            link(dve.tensor_tensor(ds, ds, mask[:, :, :], ALU.mult))
            link(dve.tensor_scalar(ds, ds, -1.0, None, ALU.add))
            link(dve.scalar_tensor_tensor(sh[:, :], incl[:, NE - 1:NE], float(P), m.cst[:, C_SLOT + 1:C_SLOT + 2], ALU.mult, ALU.add))
            link(dve.tensor_scalar(m.dest[:, :, NE], m.cst[:, C_TOK:C_TOK + NT], sh[:, :], None, ALU.add))
            link(dve.memset(m.w3[:, :, NE, :], 0.0))
            link(dve.memset(m.w3[:, :, NE, 0:1], 1.0))
            link(dve.tensor_copy(m.tab[:, 2 * P:2 * P + NE], incl[0:1, :]))
            last = m.tab[:, 2 * P + NE:2 * P + NE + 1]
            link(dve.tensor_scalar(last, incl[0:1, NE - 1:NE], float(NT + 1), None, ALU.add))
            link(dve.tensor_scalar(last, last, 1, None, ALU.logical_shift_right))
            for t in range(NT):
                link(dve.tensor_copy(m.tok[:, t, 0:1], m.cst[:, C_SLOT + 2:C_SLOT + 3]))
            link(dve.tensor_copy(m.tok[:, :, 1], m.cst[:, C_TOK:C_TOK + NT]))
            link(dve.memset(m.tok[:, :, 2:3], 1.0))


def stage_experts(nc, a, m):
    with ExitStack() as ctx:
        sb = lambda name, shape, dt=F32: ctx.enter_context(nc.sbuf_tensor(name, shape, dt))
        sem = lambda name: ctx.enter_context(nc.semaphore(name))
        w13 = sb("w13", [P, WSLOT, 2, KT, DE])
        w2 = sb("w2", [P, WSLOT, 2, D])
        xg = [sb(f"xg{j}", [P, D]) for j in range(2)]
        xT = [[sb(f"xT{part}{j}", [P, KT, P], F32R) for part in "hl"] for j in range(2)]
        wup = [[sb(f"wup{part}{j}", [P, 2, KT, DE], F32R) for part in "hl"] for j in range(2)]
        onehot = [sb(f"onehot{j}", [P, NT, P], BF16) for j in range(2)]
        parts = [sb(f"parts{j}", [P, NT, 6], BF16) for j in range(2)]
        base, dcol = sb("base", [P, 1]), sb("dcol", [P, NT])
        fx = sb("fx", [P, 4])
        idx_g, idx_s = [sb(f"idx_g{j}", [P, 1], I32) for j in range(2)], [sb(f"idx_s{j}", [P, 1], I32) for j in range(2)]
        lst_new, lst = [sb(f"lst_new{j}", [P, 2]) for j in range(2)], [sb(f"lst{j}", [P, 2]) for j in range(2)]
        hs, hb = [sb(f"hs{j}", [P, DE]) for j in range(2)], [sb(f"hb{j}", [P, DE]) for j in range(2)]
        hT = sb("hT5", [P, 2, P])
        y = [sb(f"y{j}", [P, D]) for j in range(2)]
        b_list, b_turn, b_up, b_h, b_down = m.banks[0], m.banks[1:3], m.banks[3:5], m.banks[5], m.banks[6:8]
        dch = sem("dve_chain5")
        s_w, s_w2 = [sem(f"ld_w{j}") for j in range(WSLOT)], [sem(f"ld_w2_{j}") for j in range(WSLOT)]
        w2_ready = sem("down_weights_in")
        w_ready, marked, listed, fixed, turned, xt_ready, up_done, act_done, h_done = (sem(n) for n in (
            "weights_in", "onehot_ready", "list_summed", "list_ready", "turned", "xT_ready", "up_done",
            "silu_done", "h_ready"))
        ht_out, ht_ready, down_done, y_act, scattered, scatter_done, copied, pool_step = (sem(n) for n in (
            "h_turned", "hT_ready", "down_done", "y_copied", "scattered", "scatter_done", "list_kept", "pool_step"))
        gathered = [sem(f"gathered{j}") for j in range(2)]
        w1 = a["exp_w1"][0].rearrange("e (p k) n -> e p k n", k=KT)
        w3 = a["exp_w3"][0].rearrange("e (p k) n -> e p k n", k=KT)
        wd = a["exp_w2"][0].rearrange("e (p j) n -> e p j n", j=2)
        w_high, w_low1, w_low3, xt_low = (sem(n) for n in ("w_high", "w1_low", "w3_low", "xT_low"))
        HALVES = [slice(0, 1), slice(1, 2)]
        block = ctx.enter_context(nc.Block())


        def entry(eng, i, hi, lo=0):
            return eng.value_load(m.tab[0:1, i], min_val=lo, max_val=hi)

        def pairs(eng):
            return eng.value_load(m.tab[0:1, 2 * P + NE:2 * P + NE + 1], min_val=1, max_val=TABLE // 2)

        def raw13(slot, half):
            return w13[:, bass.ds(slot, 1), half, :, :].rearrange("p s w k n -> p (s w) (k n)")

        def part13(w, half):
            return w[:, half, :, :].rearrange("p w k n -> p w (k n)")

        def low_part(eng, b, j, i, done):
            e = expert(eng, b)
            eng.wait_ge(w_ready, e + 1)
            if not (isinstance(b, int) and b < 2):
                eng.wait_ge(up_done, b - 1)
            eng.wait_ge(w_high, 2 * b + (i + 1))
            half = HALVES[i]
            eng.tensor_tensor(part13(wup[j][1], half), raw13(e % WSLOT, half),
                              part13(wup[j][0], half).bitcast(F32), ALU.subtract).then_inc(done, 1)

        def expert(eng, b):
            return entry(eng, bass.ds(b, 1), NE)

        @block.sync
        def _(sp):
            def up_weights(e, r=None):
                slot = e % WSLOT
                if r is not None:
                    x = bass.ds(r * WSLOT + e, 1)
                    p1, p3 = (w[x].rearrange("e p k n -> (e p) k n") for w in (w1, w3))
                elif e < NE:
                    p1, p3 = w1[e], w3[e]
                else:
                    p1, p3 = (a[n][0].rearrange("(p k) n -> p k n", k=KT) for n in ("shared_w1", "shared_w3"))
                sp.dma_start(w13[:, slot, 0, :, :], p1).then_inc(s_w[slot], 16)
                sp.dma_start(w13[:, slot, 1, :, :], p3).then_inc(s_w[slot], 16)

            def down_weights(e, r=None):
                if r is not None:
                    p2 = wd[bass.ds(r * WSLOT + e, 1)].rearrange("e p j n -> (e p) j n")
                elif e < NE:
                    p2 = wd[e]
                else:
                    p2 = a["shared_w2"][0].rearrange("(p j) n -> p j n", j=2)
                sp.dma_start(w2[:, e % WSLOT, :, :], p2).then_inc(s_w2[e % WSLOT], 16)

            def ends(e, r=None):
                at = 2 * P + e
                return entry(sp, slice(at, at + 1) if r is None else bass.ds(r * WSLOT + at, 1), TABLE, 1)

            def next_up(e, n, r=None):
                before = ends(e - WSLOT, r)
                sp.wait_ge(w_low1, before)
                sp.wait_ge(w_low3, before)
                up_weights(e, r)
                sp.wait_ge(s_w[e % WSLOT], 32 * n)
                sp.sem_inc(w_ready, 1)

            def next_down(e, n, r=None):
                sp.wait_ge(down_done, ends(e - WSLOT, r))
                down_weights(e, r)
                sp.wait_ge(s_w2[e % WSLOT], 16 * n)
                sp.sem_inc(w2_ready, 1)

            for e in range(WSLOT):
                up_weights(e)
            for e in range(WSLOT):
                down_weights(e)
            for e in range(WSLOT):
                sp.wait_ge(s_w[e], 32)
                sp.sem_inc(w_ready, 1)
            for e in range(WSLOT):
                sp.wait_ge(s_w2[e], 16)
                sp.sem_inc(w2_ready, 1)
            for e in range(WSLOT, 2 * WSLOT):
                next_up(e, 2)
                if e > WSLOT:
                    next_down(e - 1, 2)
            FULL = NE // WSLOT
            with sp.Fori(2, FULL) as r:
                for e in range(WSLOT):
                    next_up(e, r + 1, r)
                    next_down(e - 1, r + (1 if e else 0), r)
            for e in range(FULL * WSLOT, NX):
                next_up(e, e // WSLOT + 1)
                next_down(e - 1, (e - 1) // WSLOT + 1)
            next_down(NE, NE // WSLOT + 1)

        @block.gpsimd
        def _(pool):
            def hold(s, value):
                pool.wait_ge(s, value)
                pool.sem_inc(pool_step, 1)

            def gather(b, j, first=False):
                hold(fixed, b + 1)
                if not first:
                    hold(turned, b - 1)
                pool.indirect_dma_start(xg[j][:, :], None, m.hn2, bass.IndirectOffsetOnAxis(ap=idx_g[j][:, :], axis=0)).then_inc(gathered[j], 16)

            def low(b, j):
                low_part(pool, b, j, 1, w_low3)

            def scatter(b, j):
                if not (isinstance(b, int) and b == 0):
                    hold(scattered, b * 16)
                    pool.sem_inc(scatter_done, 1)
                hold(y_act, b + 2)
                pool.indirect_dma_start(m.yacc, bass.IndirectOffsetOnAxis(ap=idx_s[j][:, :], axis=0), y[j][:, :], None,
                                        compute_op=ALU.add).then_inc(scattered, 16)

            n = pairs(pool)
            pool.sem_inc(scatter_done, 2)
            gather(0, 0, True)
            low(0, 0)
            gather(1, 1, True)
            low(1, 1)
            gather(2, 0)
            gather(3, 1)
            for u in range(2):
                low(u + 2, u)
                gather(u + 4, u)
                scatter(u, u)
            with pool.Fori(1, n) as r:
                for u in range(2):
                    low(r * 2 + (u + 2), u)
                    gather(r * 2 + (u + 4), u)
                    scatter(r * 2 + u, u)
            hold(scattered, n * 32)
            hold(gathered[0], n * 16 + 32)
            hold(gathered[1], n * 16 + 32)

        @block.tensor
        def _(pe):
            def lists(b, j):
                pe.wait_ge(marked, b + 1)
                if not (isinstance(b, int) and b == 0):
                    pe.wait_ge(fixed, b)
                for t in range(NT):
                    mm = pe.matmul(b_list[:, 0:6], onehot[j][:, t, :], parts[j][:, t, :], start=(t == 0), stop=(t == NT - 1))
                mm.then_inc(listed, 1)

            def turn(b, j):
                pe.wait_ge(gathered[j], (b // 2) * 16 + 16)
                if not (isinstance(b, int) and b == 0):
                    pe.wait_ge(xt_low, b)
                for k in range(KT):
                    mm = pe.transpose(b_turn[k // 4][:, (k % 4) * P:(k % 4 + 1) * P], xg[j][:, k:D:KT], m.ident)
                mm.then_inc(turned, 1)

            def up(b, j):
                pe.wait_ge(w_high, 2 * (b + 1))
                pe.wait_ge(w_low1, b + 1)
                pe.wait_ge(w_low3, b + 1)
                pe.wait_ge(xt_ready, b + 1)
                pe.wait_ge(xt_low, b + 1)
                if not (isinstance(b, int) and b < 2):
                    pe.wait_ge(h_done, b)
                (xh, xl), (wh, wl) = xT[j], wup[j]
                for k in range(KT):
                    for i, (x, w) in enumerate(((xh, wh), (xh, wl), (xl, wh))):
                        mm = pe.matmul(b_up[j][:, :], x[:, k, :], w[:, :, k, :],
                                       start=(k == 0 and i == 0), stop=(k == KT - 1 and i == 2))
                mm.then_inc(up_done, 1)

            def turn_h(b, j):
                pe.wait_ge(h_done, b + 2)
                for i in range(2):
                    mm = pe.transpose(b_h[:, i * P:(i + 1) * P], hb[j][:, i:DE:2], m.ident)
                mm.then_inc(ht_out, 1)

            def down(b, j):
                e = expert(pe, b)
                slot = e % WSLOT
                pe.wait_ge(w2_ready, e + 1)
                pe.wait_ge(ht_ready, b + 1)
                pe.wait_ge(y_act, b + 1)
                for half in range(2):
                    for i in range(2):
                        mm = pe.matmul(b_down[half][:, :], hT[:, i, :],
                                       w2[:, bass.ds(slot, 1), i, half * 512:(half + 1) * 512].rearrange("p s n -> p (s n)"),
                                       start=(i == 0), stop=(i == 1))
                mm.then_inc(down_done, 1)

            n = pairs(pe)
            pe.sem_inc(ht_out, 1)
            lists(0, 0)
            lists(1, 1)
            lists(2, 0)
            turn(0, 0)
            lists(3, 1)
            turn(1, 1)
            up(0, 0)
            with pe.Fori(0, n) as r:
                for u in range(2):
                    turn_h(r * 2 + u, u)
                    lists(r * 2 + (u + 4), u)
                    up(r * 2 + (u + 1), 1 - u)
                    turn(r * 2 + (u + 2), u)
                    down(r * 2 + u, u)

        @block.scalar
        def _(act):
            def xt(b, j):
                act.wait_ge(turned, b + 1)
                if not (isinstance(b, int) and b < 2):
                    act.wait_ge(up_done, b - 1)
                act.activation(xT[j][0][:, 0:4, :], b_turn[0][:, :].rearrange("p (k n) -> p k n", k=4), ACT.Copy)
                act.activation(xT[j][0][:, 4:8, :], b_turn[1][:, :].rearrange("p (k n) -> p k n", k=4), ACT.Copy).then_inc(xt_ready, 1)

            def silu(b, j):
                act.wait_ge(up_done, b + 1)
                if not (isinstance(b, int) and b < 2):
                    act.wait_ge(h_done, b)
                act.activation(hs[j][:, :], b_up[j][:, 0:DE], ACT.Silu).then_inc(act_done, 1)

            def ht(b):
                act.wait_ge(ht_out, b + 2)
                act.activation(hT[:, :, :], b_h[:, 0:DE].rearrange("p (i n) -> p i n", i=2), ACT.Copy).then_inc(ht_ready, 1)

            def y_half(b, j):
                act.wait_ge(down_done, b + 1)
                act.wait_ge(copied, b + 1)
                act.activation(y[j][:, 0:512], b_down[0][:, :], ACT.Copy)
                act.activation(y[j][:, 512:1024], b_down[1][:, :], ACT.Copy).then_inc(y_act, 1)

            def high(b, j):
                e = expert(act, b)
                act.wait_ge(w_ready, e + 1)
                if not (isinstance(b, int) and b < 2):
                    act.wait_ge(up_done, b - 1)
                for half in HALVES:
                    act.activation(part13(wup[j][0], half), raw13(e % WSLOT, half), ACT.Copy).then_inc(w_high, 1)

            n = pairs(act)
            act.sem_inc(y_act, 1)
            high(0, 0)
            xt(0, 0)
            xt(1, 1)
            high(1, 1)
            silu(0, 0)
            with act.Fori(0, n) as r:
                for u in range(2):
                    ht(r * 2 + u)
                    high(r * 2 + (u + 2), u)
                    silu(r * 2 + (u + 1), 1 - u)
                    xt(r * 2 + (u + 2), u)
                    y_half(r * 2 + u, u)

        @block.vector
        def _(dve):
            BODY = 8

            def mark(b, j, link):
                e = bass.ds(expert(dve, b), 1)
                if not (isinstance(b, int) and b == 0):
                    dve.wait_ge(marked, b)
                if not (isinstance(b, int) and b < 2):
                    dve.wait_ge(listed, b - 1)
                link(dve.tensor_scalar(dcol[:, :], m.dest[:, :, e].rearrange("p t e -> p (t e)"), base[:, :], None, ALU.subtract))
                link(dve.tensor_scalar(base[:, :], base[:, :], float(P), None, ALU.add))
                link(dve.tensor_copy(parts[j][:, :, 3:6], m.w3[:, :, e, :].rearrange("p t e w -> p (t e) w")))
                dve.tensor_tensor(onehot[j][:, :, :], m.iota.unsqueeze(1).to_broadcast([P, NT, P]),
                                  dcol[:, :].unsqueeze(2).to_broadcast([P, NT, P]), ALU.is_equal).then_inc(marked, 1)

            def fix(b, j, link):
                dve.wait_ge(listed, b + 1)
                link(dve.tensor_copy(fx[:, 0:3], b_list[:, 0:3]))
                link(dve.scalar_tensor_tensor(fx[:, 0:1], fx[:, 2:3], m.cst[:, C_SLOT:C_SLOT + 1], fx[:, 0:1], ALU.mult, ALU.add))
                link(dve.scalar_tensor_tensor(lst_new[j][:, 0:1], fx[:, 1:2], m.cst[:, C_SLOT + 1:C_SLOT + 2], fx[:, 0:1], ALU.add, ALU.add))
                link(dve.reduce_sum(lst_new[j][:, 1:2], b_list[:, 3:6], AX))
                if not (isinstance(b, int) and b < 2):
                    dve.wait_ge(gathered[j], (b // 2) * 16)
                dve.tensor_copy(idx_g[j][:, :], lst_new[j][:, 0:1]).then_inc(fixed, 1)

            def keep(b, j, link):
                link(dve.tensor_copy(lst[j][:, :], lst_new[j][:, :]))

            def rows(b, j):
                dve.wait_ge(scatter_done, b + 1)
                dve.tensor_copy(idx_s[j][:, :], lst[j][:, 0:1]).then_inc(copied, 1)
                dve.wait_ge(copied, b + 1)

            def hidden(b, j):
                dve.wait_ge(act_done, b + 1)
                if not (isinstance(b, int) and b < 2):
                    dve.wait_ge(ht_out, b)
                dve.scalar_tensor_tensor(hb[j][:, :], hs[j][:, :], lst[j][:, 1:2], b_up[j][:, DE:2 * DE], ALU.mult, ALU.mult).then_inc(h_done, 1)

            def low(b, j):
                low_part(dve, b, j, 0, w_low1)

            def x_low(b, j):
                dve.wait_ge(xt_ready, b + 1)
                if not (isinstance(b, int) and b < 2):
                    dve.wait_ge(up_done, b - 1)
                for i in range(2):
                    ins = dve.tensor_tensor(xT[j][1][:, 4 * i:4 * i + 4, :], b_turn[i][:, :].rearrange("p (k n) -> p k n", k=4),
                                            xT[j][0][:, 4 * i:4 * i + 4, :].bitcast(F32), ALU.subtract)
                ins.then_inc(xt_low, 1)

            link = Chain(dve, dch)
            dve.sem_inc(h_done, 1)
            link(dve.memset(base[:, :], 0.0))
            for j in range(2):
                link(dve.tensor_copy(parts[j][:, :, 0:3], m.tok[:, :, :]))
            mark(0, 0, link)
            mark(1, 1, link)
            for j in range(2):
                fix(j, j, link)
                keep(j, j, link)
                mark(j + 2, j, link)
            low(0, 0)
            x_low(0, 0)
            fix(2, 0, link)
            mark(4, 0, link)
            fix(3, 1, link)
            x_low(1, 1)
            low(1, 1)
            hidden(0, 0)
            done = link.n
            n = pairs(dve)
            with dve.Fori(0, n) as r:
                inner = LoopChain(dve, dch, done, r, 2 * BODY)
                for u in range(2):
                    rows(r * 2 + u, u)
                    keep(r * 2 + (u + 2), u, inner)
                    fix(r * 2 + (u + 4), u, inner)
                    low(r * 2 + (u + 2), u)
                    mark(r * 2 + (u + 5), 1 - u, inner)
                    hidden(r * 2 + (u + 1), 1 - u)
                    x_low(r * 2 + (u + 2), u)
                assert inner.n == 2 * BODY


class LoopChain:

    def __init__(self, eng, sem, before, it, per):
        self.eng, self.sem, self.before, self.it, self.per, self.n = eng, sem, before, it, per, 0

    def __call__(self, ins):
        self.n += 1
        ins.then_inc(self.sem, 1)
        self.eng.wait_ge(self.sem, self.it * self.per + (self.before + self.n))


def stage_final(nc, a, o, m):
    with ExitStack() as ctx:
        sb = lambda name, shape, dt=F32: ctx.enter_context(nc.sbuf_tensor(name, shape, dt))
        sem = lambda name: ctx.enter_context(nc.semaphore(name))
        gate = [sb(f"gate6_{s}", [P, D]) for s in range(2)]
        nfrow, sq = sb("nfrow", [P, D]), sb("sq6", [P, D])
        x, y = [sb(f"x6_{j}", [P, D]) for j in range(3)], [sb(f"y6_{j}", [P, D]) for j in range(3)]
        ss, rs, rt = sb("ss6", [P, NT]), sb("rs6", [P, 1]), sb("rt6", [P, 1])
        ri = sb("ri6", [P, 1], I32)
        s_in, s_x, s_out = sem("ld_final"), [sem(f"ld_x6_{j}") for j in range(3)], [sem(f"st_y{j}") for j in range(3)]
        dch, x_new, x_sq, y_new = (sem(n) for n in ("dve_chain6", "x3_new", "x3_sq", "y_new"))
        block = ctx.enter_context(nc.Block())

        @block.sync
        def _(sp):
            for s in range(2):
                sp.dma_start(gate[s][:, :], m.mods[s:s + 1, 5 * D:6 * D].to_broadcast([P, D])).then_inc(s_in, 16)
            sp.dma_start(nfrow[:, :], a["norm_final"].unsqueeze(0).to_broadcast([P, D])).then_inc(s_in, 16)
            for t in range(NT):
                if t >= 3:
                    sp.wait_ge(s_out[t % 3], 16 * (t // 3))
                sp.dma_start(x[t % 3][:, :], m.x2[t * P:(t + 1) * P, :]).then_inc(s_x[t % 3], 16)
                sp.dma_start(y[t % 3][:, :], m.yacc[t * P:(t + 1) * P, :]).then_inc(s_x[t % 3], 16)

        @block.gpsimd
        def _(pool):
            for t in range(NT):
                pool.wait_ge(y_new, t + 1)
                dst = o[0][0] if t == 0 else o[1][0, (t - 1) * P:t * P, :]
                pool.dma_start(dst, x[t % 3][:, :]).then_inc(s_out[t % 3], 16)
            for j in range(3):
                pool.wait_ge(s_out[j], 16 * ((NT + 2 - j) // 3))

        @block.scalar
        def _(act):
            for t in range(NT):
                act.wait_ge(x_new, t + 1)
                if t >= 1:
                    act.wait_ge(x_sq, t)
                act.activation(sq[:, :], x[t % 3][:, :], ACT.Square, accum_out=ss[:, t:t + 1]).then_inc(x_sq, 1)

        @block.vector
        def _(dve):
            link = Chain(dve, dch)

            def add(t):
                dve.wait_ge(s_x[t % 3], 32 * (t // 3 + 1))
                yt, xt = y[t % 3][:, :], x[t % 3][:, :]
                link(dve.tensor_tensor(yt, yt, gate[min(t, 1)][:, :], ALU.mult))
                dve.tensor_tensor(xt, xt, yt, ALU.add).then_inc(x_new, 1)

            dve.wait_ge(s_in, 48)
            add(0)
            for t in range(NT):
                if t + 1 < NT:
                    add(t + 1)
                dve.wait_ge(x_sq, t + 1)
                v = ss[:, t:t + 1]
                link(dve.tensor_scalar(v, v, 1.0 / D, EPS, ALU.mult, ALU.add))
                newton_rsqrt(link, dve, v, rs[:, :], rt[:, :], ri[:, :])
                dve.scalar_tensor_tensor(x[t % 3][:, :], x[t % 3][:, :], rs[:, :], nfrow[:, :], ALU.mult, ALU.mult).then_inc(y_new, 1)


INPUTS = ["x_prompt", "x_sample", "c", "state_mlstm_C", "state_mlstm_n", "state_mlstm_m", "state_rglru_h", "c_ctx",
          "w_ada", "b_ada", "norm1", "w_in", "mlstm_gate_bias", "mlstm_norm", "rg_conv_w", "rg_conv_b", "rg_wa", "rg_ba",
          "rg_wx", "rg_bx", "rg_lambda", "rg_norm", "w_out", "norm2", "router_w", "router_bias", "exp_w1", "exp_w3",
          "exp_w2", "shared_w1", "shared_w3", "shared_w2", "norm_final"]
OUTPUTS = [(1, NCTX, D), (1, NLAT, D), (1, 1, 2, H, P, P), (1, 1, 2, H, P), (1, 1, 2, H), (1, 1, 2, DRG)]


def program(nc, a, o):
    m = Bag()
    with ExitStack() as ctx:
        sb = lambda name, shape, dt=F32: ctx.enter_context(nc.sbuf_tensor(name, shape, dt))
        sem = lambda name: ctx.enter_context(nc.semaphore(name))
        dram = lambda name, shape: nc.dram_tensor(name, shape, F32, kind="Internal").ap()
        m.mods, m.x1, m.x2 = dram("mods_scratch", (2, 6 * D)), dram("x1_scratch", (N, D)), dram("x2_scratch", (N, D))
        m.hn2, m.yacc = dram("hn2_scratch", (ROWS, D)), dram("yacc_scratch", (ROWS, D))
        m.banks = [ctx.enter_context(nc.psum_tensor(f"bank{j}", [P, 512], F32)) for j in range(8)]
        m.ring = m.banks[0:2]
        m.cst = sb("cst", [P, C_END])
        m.ident, m.tri, m.iota = m.cst[:, C_ID:C_ID + P], m.cst[:, C_TRI:C_TRI + P], m.cst[:, C_IOTA:C_IOTA + P]
        m.neg = [m.cst[:, C_NEGF:C_NEGF + P], m.cst[:, C_NEGB:C_NEGB + P]]
        m.sel = m.cst[0:H, C_SEL:C_SEL + H * P].rearrange("p (h t) -> p h t", h=H)
        m.ones = m.cst[:, C_ONE:C_ONE + P]
        m.epsc = m.cst[:, C_EPS:C_EPS + 1]
        m.ld = sem("ld_small")
        m.modst = [sem(f"st_mod{j}") for j in range(2)]
        shared = sb("shared", [P, 2 * N])
        m.mn = shared[0:H, :].rearrange("p (d n) -> p d n", d=2)
        nd_, nw = NT * NX, (NT * NX * 3 + 1) // 2
        m.dest = shared[:, 0:nd_].rearrange("p (t e) -> p t e", t=NT)
        m.w3 = shared[:, nd_:nd_ + nw].bitcast(BF16)[:, 0:NT * NX * 3].rearrange("p (t e w) -> p t e w", t=NT, e=NX)
        m.tab, m.tok = sb("tab", [1, 2 * P + NE + 4], I32), sb("tok", [P, NT, 3], BF16)
        with ExitStack() as mixer:
            sbm = lambda name, shape, dt=F32: mixer.enter_context(nc.sbuf_tensor(name, shape, dt))
            m.mlnc, m.rgnc, m.convb = sbm("mlnc", [P, H]), sbm("rgnc", [P, RT]), sbm("convb", [P, RT])
            m.convw, m.h0c = sbm("convw", [P, 4, RT]), sbm("h0c", [P, 2, RT])
            m.lam, m.bgate = sbm("lam", [P, 2 * RT]), sbm("bgate", [P, 2, 2, RT])
            m.gbias, m.m0 = sbm("gbias", [H, 4]), sbm("m0", [H, 2])
            m.cols, m.decb = sbm("cols", [P, 2 * NT, 4, H]), sbm("decb", [P, H, 2, NT])
            m.yT = sbm("yT", [P, KT, N])
            m.g4 = m.yT[0:H, 0:4, :]
            with ExitStack() as proj:
                m.hnT = proj.enter_context(nc.sbuf_tensor("hnT", [P, KT, N], F32))
                stage_norm1(nc, a, m)
                stage_rglru(nc, a, o, m)
                stage_mlstm(nc, a, o, m)
            stage_route(nc, a, m)
        stage_experts(nc, a, m)
        stage_final(nc, a, o, m)


def kernel(**inputs):
    import numpy as np
    from concourse import bacc
    from concourse.bass_utils import run_bass_kernel_spmd

    nc = bacc.Bacc("TRN2", target_bir_lowering=False, num_devices=1)
    consts, pos_row, pos_col = shape_constants()
    data = {name: np.ascontiguousarray(inputs[name]) for name in INPUTS}
    data.update(consts=consts, pos_row=pos_row, pos_col=pos_col)
    arrays, a = {}, {}
    for name, x in data.items():
        arrays[f"in_{name}"] = x
        a[name] = nc.dram_tensor(f"in_{name}", x.shape, mybir.dt.from_np(x.dtype), kind="ExternalInput").ap()
    o = [nc.dram_tensor(f"out_{i}", s, F32, kind="ExternalOutput").ap() for i, s in enumerate(OUTPUTS)]
    program(nc, a, o)
    r = run_bass_kernel_spmd(nc, [arrays], core_ids=[0])
    return tuple(r.results[0][f"out_{i}"] for i in range(len(OUTPUTS)))
```
